# Optimizing a Trainium2 kernel written in Bass

```python
import math
import jax, jax.numpy as jnp
from jax import lax
import numpy as np

D_MODEL = 1024
BATCH = 1
SEQ = 1024
DEPTH = 1

CHUNK = 64
Q_BLOCK = 128
RET_HEADS = 4
RET_DK = 128
RET_DV = 256
RET_QK = RET_HEADS * RET_DK
RET_V = RET_HEADS * RET_DV
FOX_HEADS = 8
FOX_DH = 128
FOX_W = FOX_HEADS * FOX_DH
D_FF = (((8 * D_MODEL + 2) // 3 + 255) // 256) * 256
ROPE_THETA = 10000.0
EPS = 1e-6
SPLIT = (RET_QK, RET_QK, RET_V, RET_V, FOX_W, FOX_W, FOX_W, FOX_HEADS, D_MODEL, D_MODEL)
D_IN = 2 * RET_QK + 2 * RET_V + 3 * FOX_W + FOX_HEADS + 2 * D_MODEL

kernel_name = "hybrid_retention_fox_gated_block"

def rms_norm(x, w):
    xf = x.astype(jnp.float32)
    y = xf * lax.rsqrt(jnp.mean(xf * xf, axis=-1, keepdims=True) + EPS)
    return (y * w.astype(jnp.float32)).astype(x.dtype)

def modulate(h, shift, scale):
    return h * (1.0 + scale[:, None, :]) + shift[:, None, :]

def rotary(x, pos):
    half = x.shape[-1] // 2
    freqs = ROPE_THETA ** (-jnp.arange(half, dtype=jnp.float32) / half)
    ang = pos.astype(jnp.float32)[:, None] * freqs[None, :]
    cos = jnp.cos(ang)[None, :, None, :]
    sin = jnp.sin(ang)[None, :, None, :]
    xf = x.astype(jnp.float32)
    x1, x2 = xf[..., :half], xf[..., half:]
    return jnp.concatenate([x1 * cos - x2 * sin, x1 * sin + x2 * cos], axis=-1).astype(x.dtype)

def retention(q, k, v):
    B, S, H, dk = q.shape
    dv = v.shape[-1]
    N = S // CHUNK
    log_gamma = jnp.log(1.0 - jnp.exp2(-5.0 - jnp.arange(H, dtype=jnp.float32)))
    qc = q.astype(jnp.float32).reshape(B, N, CHUNK, H, dk)
    kc = k.astype(jnp.float32).reshape(B, N, CHUNK, H, dk)
    vc = v.astype(jnp.float32).reshape(B, N, CHUNK, H, dv)
    idx = jnp.arange(CHUNK, dtype=jnp.float32)
    d_intra = jnp.exp(log_gamma[:, None, None] * jnp.abs(idx[:, None] - idx[None, :]))
    scores = jnp.einsum('bnihd,bnjhd->bnhij', qc, kc) * d_intra
    intra = jnp.einsum('bnhij,bnjhe->bnihe', scores, vc)
    k_dec = jnp.exp(log_gamma[None, :] * (CHUNK - idx)[:, None])
    summ = jnp.einsum('bnjhd,bnjhe->bnhde', kc * k_dec[None, None, :, :, None], vc)
    chunk_decay = jnp.exp(log_gamma * CHUNK)[None, :, None, None]

    def step(state, a):
        return chunk_decay * state + a, state

    _, s_in = lax.scan(step, jnp.zeros((B, H, dk, dv), jnp.float32), jnp.moveaxis(summ, 1, 0))
    s_in = jnp.moveaxis(s_in, 0, 1)
    q_dec = jnp.exp(log_gamma[None, :] * idx[:, None])
    inter = jnp.einsum('bnihd,bnhde->bnihe', qc * q_dec[None, None, :, :, None], s_in)
    return (intra + inter).reshape(B, S, H, dv)

def forgetting_attention(q, k, v, log_f):
    B, S, H, d = q.shape
    nq = S // Q_BLOCK
    scale = 1.0 / math.sqrt(d)
    F = jnp.cumsum(log_f, axis=1).transpose(0, 2, 1)
    kt = k.transpose(0, 2, 1, 3)
    vt = v.transpose(0, 2, 1, 3)
    qb = jnp.moveaxis(q.transpose(0, 2, 1, 3).reshape(B, H, nq, Q_BLOCK, d), 2, 0)
    Fqb = jnp.moveaxis(F.reshape(B, H, nq, Q_BLOCK), 2, 0)
    kpos = jnp.arange(S)
    posb = kpos.reshape(nq, Q_BLOCK)

    def block(args):
        qi, fi, pi = args
        s = jnp.einsum('bhqd,bhkd->bhqk', qi, kt).astype(jnp.float32) * scale
        s = s + fi[..., :, None] - F[:, :, None, :]
        s = jnp.where((pi[:, None] >= kpos[None, :])[None, None], s, -jnp.inf)
        p = jax.nn.softmax(s, axis=-1)
        return jnp.einsum('bhqk,bhkd->bhqd', p.astype(vt.dtype), vt)

    out = lax.map(block, (qb, Fqb, posb))
    out = jnp.moveaxis(out, 0, 2).reshape(B, H, S, d).transpose(0, 2, 1, 3)
    return out.reshape(B, S, H * d)

def setup_inputs(seed: int = 0) -> dict:
    key = jax.random.key(seed)
    ks = jax.random.split(key, 16)
    f32 = jnp.float32
    L, D = DEPTH, D_MODEL
    nrm = lambda k, shape, fan: jax.random.normal(k, shape, f32) * (fan ** -0.5)
    return {
        "x": jax.random.normal(ks[0], (BATCH, SEQ, D), f32),
        "c": jax.random.normal(ks[1], (BATCH, D), f32),
        "ada_w": nrm(ks[2], (L, D, 6 * D), D) * 0.5,
        "ada_b": 0.01 * jax.random.normal(ks[3], (L, 6 * D), f32),
        "norm1_w": 1.0 + 0.01 * jax.random.normal(ks[4], (L, D), f32),
        "w_in": nrm(ks[5], (L, D, D_IN), D),
        "b_f": 1.0 + 3.0 * jax.random.uniform(ks[6], (L, FOX_HEADS), f32),
        "ret_proj": nrm(ks[7], (L, RET_V, D), RET_V),
        "fox_proj": nrm(ks[8], (L, FOX_W, D), FOX_W),
        "w_out": nrm(ks[9], (L, D, D), D),
        "norm2_w": 1.0 + 0.01 * jax.random.normal(ks[10], (L, D), f32),
        "w_gate": nrm(ks[11], (L, D, D_FF), D),
        "w_up": nrm(ks[12], (L, D, D_FF), D),
        "w_down": nrm(ks[13], (L, D_FF, D), D_FF),
        "norm_f_w": 1.0 + 0.01 * jax.random.normal(ks[14], (D,), f32),
    }

def reference(x, c, ada_w, ada_b, norm1_w, w_in, b_f, ret_proj, fox_proj, w_out,
              norm2_w, w_gate, w_up, w_down, norm_f_w):
    B, S, D = x.shape
    pos = jnp.arange(S)
    offs = [int(o) for o in np.cumsum(SPLIT)[:-1]]
    c_act = jax.nn.silu(c)
    for l in range(DEPTH):
        mod = c_act @ ada_w[l] + ada_b[l]
        sh1, sc1, g1, sh2, sc2, g2 = jnp.split(mod, 6, axis=-1)

        h = modulate(rms_norm(x, norm1_w[l]), sh1, sc1)
        z = h @ w_in[l]
        rq, rk, rv, rg, fq, fk, fv, ff, gr, gf = jnp.split(z, offs, axis=-1)

        rq = rotary(rq.reshape(B, S, RET_HEADS, RET_DK), pos)
        rk = rotary(rk.reshape(B, S, RET_HEADS, RET_DK), pos) * (RET_DK ** -0.5)
        ro = retention(rq, rk, rv.reshape(B, S, RET_HEADS, RET_DV))
        ro = ro * lax.rsqrt(jnp.mean(ro * ro, axis=-1, keepdims=True) + EPS)
        y_ret = (jax.nn.silu(rg.astype(jnp.float32)) * ro.reshape(B, S, RET_V)).astype(x.dtype)

        log_f = jax.nn.log_sigmoid((ff + b_f[l]).astype(jnp.float32))
        y_fox = forgetting_attention(fq.reshape(B, S, FOX_HEADS, FOX_DH),
                                     fk.reshape(B, S, FOX_HEADS, FOX_DH),
                                     fv.reshape(B, S, FOX_HEADS, FOX_DH), log_f)

        merged = jax.nn.sigmoid(gr) * (y_ret @ ret_proj[l]) + jax.nn.sigmoid(gf) * (y_fox @ fox_proj[l])
        x = x + g1[:, None, :] * (merged @ w_out[l])

        h2 = modulate(rms_norm(x, norm2_w[l]), sh2, sc2)
        ffn = (jax.nn.silu(h2 @ w_gate[l]) * (h2 @ w_up[l])) @ w_down[l]
        x = x + g2[:, None, :] * ffn
    return rms_norm(x, norm_f_w)


_drawn_inputs = setup_inputs


def setup_inputs(seed=0):
    import zlib

    import numpy as np

    out = dict(_drawn_inputs(seed))
    spreads = {}
    factors = {'ada_b': 5.68, 'norm1_w': 8.0, 'norm2_w': 8.0, 'norm_f_w': 5.761}
    for name, (base, spread) in spreads.items():
        noise = np.random.default_rng([zlib.crc32(name.encode()), seed]).standard_normal(out[name].shape)
        drawn = base * np.exp(spread * noise) if base else spread * noise
        out[name] = __import__('jax').numpy.asarray(drawn.astype(out[name].dtype))
    for name, factor in factors.items():
        out[name] = (out[name] * factor).astype(out[name].dtype)
    return out
```

```python
import concourse.bass as bass
from concourse import mybir
from contextlib import ExitStack
import numpy as np

F32 = mybir.dt.float32
F32R = mybir.dt.float32r
ALU = mybir.AluOpType
ACT = mybir.ActivationFunctionType

P = 128
D = 1024
S = 1024
KT = D // P
TT = S // P
HALF = 512
RH, DK, DV, CHUNK = 4, 128, 256, 64
FH, DH = 8, 128
D_FF = (((8 * D + 2) // 3 + 255) // 256) * 256
EPS = 1e-6
RET_QK, RET_V, FOX_W = RH * DK, RH * DV, FH * DH
(O_RQ, O_RK, O_RV, O_RG, O_FQ, O_FK, O_FV, O_FF, O_GR, O_GF) = np.cumsum(
    [0, RET_QK, RET_QK, RET_V, RET_V, FOX_W, FOX_W, FOX_W, FH, D]).tolist()
NEG = -(2.0 ** 100)
FF_PAIRS = D_FF // (2 * P)

RET_TILES = 8
T_RET = 0
T_FF = T_RET + RET_TILES * RH
T_FOX = T_FF + 3
FOX_TILES = 4
T_WO = T_FOX + FOX_TILES * (FH - 1) + 2
PAIR_TILES = 6
T_FFN = T_WO + PAIR_TILES * (D // (2 * P))

RC = P + 4


def host_constants():
    half = DK // 2
    freqs = np.float32(10000.0) ** (-np.arange(half, dtype=np.float32) / np.float32(half))
    ang = np.arange(S, dtype=np.float32)[None, :] * freqs.astype(np.float32)[:, None]
    cos, sin = np.cos(ang), np.sin(ang)
    rope = np.stack([np.concatenate([cos, cos]), np.concatenate([-sin, sin])], 1)
    ident = np.eye(P)
    s, t = np.arange(P)[:, None], np.arange(P)[None, :]
    causal = np.where(t <= s, 0.0, NEG)
    ret = np.zeros((RH + 1, P, RC))
    for h in range(RH):
        lg = np.log(1.0 - 2.0 ** (-5.0 - h))
        seen = (s // CHUNK) <= (t // CHUNK)
        ret[h, :, :P] = np.where(seen, np.exp(lg * (np.abs(t - s) - t)), 0.0) * DK ** -0.5
        i = np.arange(P)
        ret[h, :, P] = np.exp(lg * (P - i)) * DK ** -0.5
        ret[h, :, P + 1] = np.exp(lg * i)
        ret[h, :, P + 2] = np.exp(2 * lg * i) / DV
        ret[h, :, P + 3] = np.exp(lg * P)
    mats = np.concatenate([ident, causal], 1)
    return {k: np.ascontiguousarray(v, dtype=np.float32)
            for k, v in {"mats": mats, "rope": rope.reshape(P, 2 * S), "ret": ret}.items()}


def hybrid_block(nc, x, c, ada_w, ada_b, norm1_w, w_in, b_f, ret_proj, fox_proj, w_out, norm2_w,
                 w_gate, w_up, w_down, norm_f_w, k_mats, k_rope, k_ret, out):
    ds = bass.ds
    x_v = x[0].rearrange("(n p) d -> p n d", p=P)
    out_v = out[0].rearrange("(n p) d -> p n d", p=P)
    ada_v = ada_w[0]
    w_in_v = w_in[0].rearrange("(k p) c -> p k c", p=P)
    gate_v = w_gate[0].rearrange("(k p) c -> p k c", p=P)
    up_v = w_up[0].rearrange("(k p) c -> p k c", p=P)
    retp, foxp, wout, wdown = ret_proj[0], fox_proj[0], w_out[0], w_down[0]

    g_rows = nc.dram_tensor("g_rows", (2, D), F32).ap()
    negf_rows = nc.dram_tensor("negf_rows", (FH, S), F32).ap()
    ret_merge = nc.dram_tensor("ret_merge", (P, KT * S), F32).ap()

    ctx = ExitStack()
    with ctx:
        def sb(name, shape, dt=F32, stack=ctx):
            return stack.enter_context(nc.sbuf_tensor("b_" + name, shape, dt))

        def sem(name):
            return ctx.enter_context(nc.semaphore(name))

        def f(ap):
            return ap.bitcast(F32)

        ps = ctx.enter_context(nc.psum_tensor("ps", [P, 8, HALF], F32))

        hT = sb("hT", [P, 2, KT, S], F32R)
        w_split = sb("w_split", [P, 2, 2, 1024], F32R)
        w_stage = sb("w_stage", [P, 2, 1024])
        macc = sb("macc", [P, KT, S])
        ident_f = sb("ident_f", [P, P])
        ident = ident_f[:, :]
        identR = sb("identR", [P, P], F32R)
        causalR = sb("causalR", [P, P], F32R)
        modT = sb("modT", [P, 48])
        nw = sb("nw", [P, 2, KT])
        amul = sb("amul", [P, KT])
        spare = sb("spare", [P, 1])
        cvec = sb("cvec", [P, KT])
        cact = sb("cact", [P, KT])
        bf = sb("bf", [FH, 1])
        stat = sb("stat", [P, 4, TT])

        st = ExitStack()
        resid0 = sb("resid0", [P, TT, D], F32, st)
        ada_ring = sb("ada_ring", [P, 4, 2048], F32, st)
        ada_acc = sb("ada_acc", [P, 2, 2048], F32, st)
        ntmp0 = sb("ntmp0", [P, 2, HALF], F32, st)
        onesf = sb("onesf", [P, P], F32, st)
        causal_f = sb("causal_f", [P, P], F32, st)
        st.close()

        st = ExitStack()
        rq2 = sb("rq2", [P, 2, S], F32R, st)
        kst = sb("kst", [P, 2, 2, S], F32R, st)
        vt_ro = sb("vt_ro", [P, 2048], F32, st)
        rv2 = sb("rv2", [P, 2, TT, DV], F32R, st)
        kd2 = sb("kd2", [P, 2, TT, DK], F32R, st)
        rm = sb("rm", [P, 2, HALF], F32, st)
        rsw = sb("rsw", [P, HALF], F32, st)
        state = sb("state", [P, DV], F32, st)
        state2 = sb("state2", [P, 3, 2, DV], F32R, st)
        gT = sb("gT", [P, 2, S], F32, st)
        rope = sb("rope", [P, 2, S], F32, st)
        rc = sb("rc", [P, RC], F32, st)
        rss = sb("rss", [P, 4, TT], F32, st)
        st.close()
        vT = vt_ro[:, :].rearrange("p (e s) -> p e s", e=2)
        ro = vt_ro[:, :].rearrange("p (b e) -> p b e", e=DV)

        st = ExitStack()
        fq2 = sb("fq2", [P, 2, S], F32R, st)
        fk2 = sb("fk2", [P, 2, S], F32R, st)
        fv2 = sb("fv2", [P, 2, TT, DH], F32R, st)
        fvT = sb("fvT", [P, S], F32, st)
        probs = sb("probs", [P, TT * (TT + 1) // 2 * P], F32, st)
        pT2 = sb("pT2", [P, 3, 2, HALF], F32R, st)
        fy2 = sb("fy2", [P, 2, S], F32R, st)
        negf = sb("negf", [P, S], F32, st)
        smax = sb("smax", [P, 5, TT], F32, st)
        st.close()
        fz = probs[0:FH, 0:4 * S].rearrange("p (a s) -> p a s", a=4)

        st = ExitStack()
        resid = sb("resid", [P, TT, D], F32, st)
        ntmp = sb("ntmp", [P, 2, HALF], F32, st)
        f2 = sb("f2", [P, 2, 2, S], F32R, st)
        ga = sb("ga", [P, 2, HALF], F32, st)
        gb = sb("gb", [P, 2, HALF], F32, st)
        fin = sb("fin", [P, 2, HALF], F32, st)
        mret = sb("mret", [P, 2, S], F32, st)
        grow = sb("grow", [P, D], F32, st)
        nfrow = sb("nfrow", [P, D], F32, st)
        st.close()

        s_const = sem("s_const")
        s_identr = sem("s_identr")
        w_loaded = [sem(f"w_loaded{i}") for i in range(2)]
        w_hi = [sem(f"w_hi{i}") for i in range(2)]
        w_ready = [sem(f"w_ready{i}") for i in range(2)]
        w_used = [sem(f"w_used{i}") for i in range(2)]
        w_g = sem("w_g")
        s_x = sem("s_x")
        s_cact = sem("s_cact")
        s_aload = [sem(f"s_aload{i}") for i in range(4)]
        s_aused = sem("s_aused")
        s_azero = sem("s_azero")
        s_abias = sem("s_abias")
        s_acc = sem("s_acc")
        s_mod = sem("s_mod")
        s_modT = sem("s_modT")
        s_row = sem("s_row")
        s_rowout = sem("s_rowout")
        s_amul = sem("s_amul")
        n_sq, n_ms, n_rt, n_r, n_xn = (sem(f"n_{k}") for k in ("sq", "ms", "rt", "r", "xn"))
        n_tr, n_tmp, n_hi, n_lo = (sem(f"n_{k}") for k in ("tr", "tmp", "hi", "lo"))
        s_mzero = sem("s_mzero")
        r_const = sem("r_const")
        r_job, r_sw, r_m, r_chain, r_rot, r_hi, r_qk = (
            sem(f"r_{k}") for k in ("job", "sw", "m", "chain", "rot", "hi", "qk"))
        r_v, r_g, r_sc, r_st, r_sthi, r_stlo = (sem(f"r_{k}") for k in ("v", "g", "sc", "st", "sthi", "stlo"))
        r_tr, r_trhi, r_trlo = (sem(f"r_{k}") for k in ("tr", "trhi", "trlo"))
        r_inc, r_state, r_stahi, r_stalo = (sem(f"r_{k}") for k in ("inc", "state", "stahi", "stalo"))
        r_out, r_ro, r_ss, r_ms, r_rt, r_rg, r_ron = (
            sem(f"r_{k}") for k in ("out", "ro", "ss", "ms", "rt", "rg", "ron"))
        r_rtr, r_ym, r_yhi, r_ylo, r_pj, r_acc = (sem(f"r_{k}") for k in ("rtr", "ym", "yhi", "ylo", "pj", "acc"))
        r_spill = sem("r_spill")
        g_job, g_z, g_abs, g_exp, g_ln, g_scan, g_store = (
            sem(f"g_{k}") for k in ("job", "z", "abs", "exp", "ln", "scan", "store"))
        a_job, a_qkhi, a_qk, a_v, a_tr, a_vhi, a_vlo = (
            sem(f"a_{k}") for k in ("job", "qkhi", "qk", "v", "tr", "vhi", "vlo"))
        a_nf, a_s, a_t, a_neg, a_e, a_r, a_p = (sem(f"a_{k}") for k in ("nf", "s", "t", "neg", "e", "r", "p"))
        a_pt, a_pthi, a_ptlo, a_pv, a_yhi, a_ylo, a_pj, a_acc = (
            sem(f"a_{k}") for k in ("pt", "pthi", "ptlo", "pv", "yhi", "ylo", "pj", "acc"))
        pair_sems = {k: {n: sem(f"{k}_{n}") for n in (
            "job", "ga", "gm", "gb", "gbm", "f", "hi", "lo", "pj", "acc", "grow")} for k in "of"}
        o_mret = [sem(f"o_mret{i}") for i in range(2)]
        s_nf = sem("s_nf")
        f_y = sem("f_y")
        f_out = sem("f_out")

        block = ctx.enter_context(nc.Block())

        def slot_turn(base, j, it=0, per=0):
            n = base + j
            return n % 2, it * (per // 2) + n // 2

        def turn_known(turn):
            return not isinstance(turn, int) or turn > 0

        @block.sync
        def _(sp):
            sp.dma_start(ident, k_mats[:, 0:P]).then_inc(s_const, 16)
            sp.dma_start(causal_f[:, :], k_mats[:, P:2 * P]).then_inc(s_const, 16)
            sp.dma_start(cvec[:, :], c).then_inc(s_const, 16)
            sp.dma_start(nw[:, 0, :], norm1_w).then_inc(s_const, 16)
            sp.dma_start(nw[:, 1, :], norm2_w).then_inc(s_const, 16)
            sp.dma_start(bf[:, :], b_f).then_inc(s_const, 16)
            for ch in range(3):
                a = ch % 2
                sp.wait_ge(s_azero, ch + 1)
                sp.dma_start(ada_acc[0:1, a, :], ada_b[0:1, ch * 2048:(ch + 1) * 2048]).then_inc(s_abias, 16)
                for k in range(KT):
                    n = ch * KT + k
                    if n >= 4:
                        sp.wait_ge(s_aused, n - 3)
                    sp.dma_start(ada_ring[:, n % 4, :],
                                 ada_v[k * P:(k + 1) * P, ch * 2048:(ch + 1) * 2048]).then_inc(s_aload[n % 4], 16)

            def load(src, base, j, it=0, per=0, cols=True):
                slot, turn = slot_turn(base, j, it, per)
                if turn_known(turn):
                    sp.wait_ge(w_ready[slot], turn)
                dst = w_stage[:, slot, :]
                if cols:
                    dst = dst.rearrange("p (k c) -> p k c", c=P)
                sp.dma_start(dst, src).then_inc(w_loaded[slot], 16)

            def retention_loads(h, base, it):
                starts = [O_RQ + h * DK, O_RK + h * DK, O_RV + h * DV, O_RV + h * DV + P,
                          O_RG + h * DV, O_RG + h * DV + P]
                for j, s0 in enumerate(starts):
                    load(w_in_v[:, :, ds(s0, P)], base, j, it, RET_TILES)
                for e in range(2):
                    load(retp[ds(h * DV + e * P, P), :], base, 6 + e, it, RET_TILES, cols=False)

            with sp.Fori(0, RH) as h:
                retention_loads(h, T_RET, h)

            for j, s0 in enumerate((O_FF, O_FQ, O_FK)):
                load(w_in_v[:, :, s0:s0 + P], T_FF, j)
            with sp.Fori(0, FH - 1) as h:
                for j, s0 in enumerate((O_FV + h * DH, O_FQ + (h + 1) * DH, O_FK + (h + 1) * DH)):
                    load(w_in_v[:, :, ds(s0, P)], T_FOX, j, h, FOX_TILES)
                load(foxp[ds(h * DH, P), :], T_FOX, 3, h, FOX_TILES, cols=False)
            last = T_FOX + FOX_TILES * (FH - 1)
            load(w_in_v[:, :, O_FV + (FH - 1) * DH:O_FV + FH * DH], last, 0)
            load(foxp[(FH - 1) * DH:FH * DH, :], last, 1, cols=False)

            def pair_loads(base, pairs, a_of, b_of, w2):
                for j, (m, e) in enumerate(((a_of, 0), (b_of, 0), (a_of, 1), (b_of, 1))):
                    load(m(e), base, j)
                with sp.Fori(0, pairs - 1) as i:
                    per = PAIR_TILES
                    load(a_of(2 * i + 2), base + 4, 0, i, per)
                    for e in range(2):
                        load(w2[ds((2 * i + e) * P, P), :], base + 4, 1 + e, i, per, cols=False)
                    load(b_of(2 * i + 2), base + 4, 3, i, per)
                    load(a_of(2 * i + 3), base + 4, 4, i, per)
                    load(b_of(2 * i + 3), base + 4, 5, i, per)
                end = base + 4 + PAIR_TILES * (pairs - 1)
                for e in range(2):
                    r = (2 * (pairs - 1) + e) * P
                    load(w2[r:r + P, :], end, e, cols=False)

            pair_loads(T_WO, KT // 2, lambda t: w_in_v[:, :, ds(O_GR + t * P, P)],
                       lambda t: w_in_v[:, :, ds(O_GF + t * P, P)], wout)
            pair_loads(T_FFN, FF_PAIRS, lambda t: gate_v[:, :, ds(t * P, P)],
                       lambda t: up_v[:, :, ds(t * P, P)], wdown)
            sp.wait_ge(s_rowout, 32)
            sp.wait_ge(r_spill, 16)
            sp.wait_ge(g_store, 16)

        @block.gpsimd
        def _(pool):
            for ch in range(3):
                if ch == 2:
                    pool.wait_ge(s_mod, 1)
                pool.memset(ada_acc[:, ch % 2, :], 0.0).then_inc(s_azero, 1)

            def split(base, j, it=0, per=0, scaled=False):
                slot, turn = slot_turn(base, j, it, per)
                src = w_stage[:, slot, :]
                hi, lo = w_split[:, slot, 0, :], w_split[:, slot, 1, :]
                pool.wait_ge(w_loaded[slot], 16 * turn + 16)
                if scaled:
                    pool.tensor_tensor(src, src, grow[:, :], ALU.mult).then_inc(w_g, 1)
                return slot, turn, src, hi, lo

            def finish(base, j, part):
                slot, turn, src, hi, lo = part
                if turn_known(turn):
                    pool.wait_ge(w_used[slot], turn)
                pool.tensor_tensor(spare[0:1, :], src[0:1, 0:1], src[0:1, 0:1], ALU.add)
                pool.tensor_scalar(hi, src, 1.0, None, ALU.mult).then_inc(w_hi[slot], 1)
                pool.wait_ge(w_hi[slot], turn + 1)
                pool.tensor_tensor(lo, src, f(hi), ALU.subtract).then_inc(w_ready[slot], 1)

            def tile(base, j, it=0, per=0):
                finish(base, j, split(base, j, it, per))

            def scaled_tile(base, j, count, it=0, per=0):
                part = split(base, j, it, per, scaled=True)
                pool.wait_ge(w_g, count)
                finish(base, j, part)

            pool.wait_ge(n_tr, 16)
            for k in range(KT):
                pool.memset(macc[:, k, :], 0.0).then_inc(s_mzero, 1)
            with pool.Fori(0, RH) as h:
                for j in range(RET_TILES):
                    tile(T_RET, j, h, RET_TILES)
            for j in range(3):
                tile(T_FF, j)
            pool.wait_ge(r_spill, 16)
            for k in range(KT):
                pool.memset(macc[:, k, :], 0.0).then_inc(s_mzero, 1)
            with pool.Fori(0, FH - 1) as h:
                for j in range(FOX_TILES):
                    tile(T_FOX, j, h, FOX_TILES)
            for j in range(2):
                tile(T_FOX + FOX_TILES * (FH - 1), j)

            def pair_splits(base, pairs, sems, scaled_before):
                for j in range(4):
                    tile(base, j)
                pool.wait_ge(sems["grow"], 16)
                with pool.Fori(0, pairs - 1) as i:
                    tile(base + 4, 0, i, PAIR_TILES)
                    for e in range(2):
                        scaled_tile(base + 4, 1 + e, scaled_before + 2 * i + e + 1, i, PAIR_TILES)
                    for j in range(3, 6):
                        tile(base + 4, j, i, PAIR_TILES)
                end = base + 4 + PAIR_TILES * (pairs - 1)
                for e in range(2):
                    scaled_tile(end, e, scaled_before + 2 * (pairs - 1) + e + 1)

            pair_splits(T_WO, KT // 2, pair_sems["o"], 0)
            pair_splits(T_FFN, FF_PAIRS, pair_sems["f"], KT)

        @block.tensor
        def _(pe):
            def mm(o, l, r, start, stop):
                return pe.matmul(o, l, r, start=start, stop=stop)

            def product(o, l, r, start, stop):
                mm(o, l[0], r[0], start, False)
                mm(o, l[0], r[1], False, False)
                return mm(o, l[1], r[0], False, stop)

            def pair(buf, cols):
                return buf[:, 0, cols], buf[:, 1, cols]

            def blk(t):
                return slice(t * P, (t + 1) * P)

            def job_part(bank, place, half, m0, m1):
                for m in range(m0, m1):
                    k, which = m // 3, m % 3
                    w = w_split[:, place[0], int(which == 2), blk(k)]
                    a = hT[:, int(which == 1), k, half * HALF:(half + 1) * HALF]
                    last = mm(ps[:, bank, :], w, a, m == 0, m == 23)
                return last

            def job_end(last, half, place, s):
                last.then_inc(s if half == 0 else w_used[place[0]], 1)

            def job(bank, place, half, s):
                if half == 0:
                    pe.wait_ge(w_ready[place[0]], place[1] + 1)
                job_end(job_part(bank, place, half, 0, 24), half, place, s)

            def norm_transposes(n):
                pe.wait_ge(n_xn, TT * (n + 1))
                for u in range(16):
                    k, half = u // 2, u % 2
                    if u >= 4:
                        pe.wait_ge(n_tmp, 16 * n + u - 3)
                    for b in range(4):
                        last = pe.transpose(ps[:, u % 4, blk(b)], macc[:, 4 * half + b, blk(k)], ident)
                    last.then_inc(n_tr, 1)

            pe.wait_ge(s_const, 96)
            pe.wait_ge(s_identr, 3)
            for ch in range(3):
                a = ch % 2
                pe.wait_ge(s_acc, ch + 1)
                if ch == 2:
                    pe.wait_ge(s_modT, 1)
                for b in range(16):
                    last = mm(ps[:, 6 + a, b:b + 1], ada_acc[:, a, blk(b)], onesf[:, 0:1], True, True)
                last.then_inc(s_mod, 1)
                if ch >= 1:
                    lo = 0 if ch == 1 else D
                    if ch == 2:
                        pe.wait_ge(s_row, 2)
                    for q in range(2):
                        last = mm(ps[:, 4 + q, :], onesf[:, :],
                                  ada_acc[:, a, lo + q * HALF:lo + (q + 1) * HALF], True, True)
                    last.then_inc(s_mod, 1)
                if ch == 0:
                    norm_transposes(0)
            pe.wait_ge(n_lo, 16)
            pe.wait_ge(s_row, 4)
            pe.wait_ge(s_modT, 3)
            pe.wait_ge(s_rowout, 32)

            with pe.Fori(0, RH) as h:
                place = [slot_turn(T_RET, j, h, RET_TILES) for j in range(RET_TILES)]

                def ret_job(j, half):
                    u = 2 * j + half
                    if u < 2:
                        pe.wait_ge(r_g, h * 4)
                    elif u < 6:
                        pe.wait_ge(r_m, h * 4 + u - 1)
                    elif u < 10:
                        pe.wait_ge(r_v, h * 4 + u - 5)
                    else:
                        pe.wait_ge(r_g, h * 4 + u - 9)
                    job(u % 2, place[j], half, r_job)

                for j in range(3):
                    ret_job(j, 0)
                    ret_job(j, 1)
                pe.wait_ge(r_qk, h * 4 + 4)
                pe.wait_ge(r_ym, h * 4)
                for q in range(2):
                    for b in range(4):
                        t = 4 * q + b
                        last = product(ps[:, 2 + q, blk(b)], pair(kst[:, 0], blk(t)), pair(rq2, blk(t)), True, True)
                    last.then_inc(r_sc, 1)
                ret_job(3, 0)
                ret_job(3, 1)
                for q in range(2):
                    pe.wait_ge(r_st, h * 2 + q + 1)
                    for b in range(4):
                        t = 4 * q + b
                        mm(ps[:, 2 + q, blk(b)], kst[:, 0, 0, blk(t)], identR[:, :], True, False)
                        last = mm(ps[:, 2 + q, blk(b)], kst[:, 0, 1, blk(t)], identR[:, :], False, True)
                    last.then_inc(r_tr, 1)
                pe.wait_ge(r_v, h * 4 + 4)
                for n in range(4):
                    e, q = n // 2, n % 2
                    pe.wait_ge(r_trlo, h * 6 + n + 1)
                    for b in range(4):
                        last = pe.transpose(ps[:, 2 + q, blk(b)], vT[:, e, blk(4 * q + b)], ident)
                    last.then_inc(r_tr, 1)

                def added(b):
                    if b == 0:
                        pe.wait_ge(r_trlo, h * 6 + 6)
                        pe.wait_ge(r_acc, h * 16)
                    if b >= 2:
                        pe.wait_ge(r_state, h * 7 + b - 1)
                    product(ps[:, 4 + b % 2, 0:DV], pair(kd2[:, :, b], slice(0, DK)),
                            pair(rv2[:, :, b], slice(0, DV)), True, True).then_inc(r_inc, 1)

                def output(b):
                    if b == 0:
                        pe.wait_ge(r_stlo, h * 2 + 2)
                    if b >= 2:
                        pe.wait_ge(r_ro, h * 8 + b - 1)
                    o = ps[:, 6 + b % 2, 0:DV]
                    last = product(o, pair(kst[:, 1], blk(b)), pair(rv2[:, :, b], slice(0, DV)), True, b == 0)
                    if b > 0:
                        pe.wait_ge(r_stalo, h * 7 + b)
                        last = product(o, pair(rq2, blk(b)), pair(state2[:, (b - 1) % 3], slice(0, DV)), False, True)
                    last.then_inc(r_out, 1)

                added(0)
                added(1)
                ret_job(4, 0)
                output(0)
                output(1)
                added(2)
                added(3)
                ret_job(4, 1)
                output(2)
                output(3)
                added(4)
                added(5)
                ret_job(5, 0)
                output(4)
                output(5)
                added(6)
                output(6)
                output(7)
                ret_job(5, 1)
                pe.wait_ge(r_ron, h + 1)
                for u in range(4):
                    e, q = u // 2, u % 2
                    if u >= 2:
                        pe.wait_ge(r_ym, h * 4 + u - 1)
                    for b in range(4):
                        last = pe.transpose(ps[:, 2 + q, blk(b)], ro[:, 4 * q + b, blk(e)], ident)
                    last.then_inc(r_rtr, 1)
                pe.wait_ge(r_ylo, h * 4 + 4)
                for slot, turn in place[6:]:
                    pe.wait_ge(w_ready[slot], turn + 1)
                for u in range(16):
                    k, q = u // 2, u % 2
                    if u >= 4:
                        pe.wait_ge(r_acc, h * 16 + u - 3)
                    for e in range(2):
                        slot = place[6 + e][0]
                        last = product(ps[:, 4 + u % 4, :], pair(w_split[:, slot], blk(k)),
                                       pair(kst[:, e], slice(q * HALF, (q + 1) * HALF)), e == 0, e == 1)
                        if u == 15:
                            last.then_inc(w_used[slot], 1)
                    if u < 15:
                        last.then_inc(r_pj, 1)

            place = [slot_turn(T_FF, j) for j in range(3)]
            pe.wait_ge(r_g, 4 * RH)
            for half in range(2):
                job(half, place[0], half, g_job)
            for j in (1, 2):
                for half in range(2):
                    if j == 1:
                        pe.wait_ge(g_z, half + 1)
                    else:
                        pe.wait_ge(a_qk, half + 1)
                    job(half, place[j], half, a_job)
            pe.wait_ge(r_ym, 4 * RH)
            pe.wait_ge(r_acc, 16 * RH)

            steps = [(0, s) for s in range(4)] + [(1, s) for s in range(8)]

            def fox_head(base, h, more):
                per = FOX_TILES
                p_v = slot_turn(base, 0, h, per)
                p_next = [slot_turn(base, 1 + j, h, per) for j in range(2)]
                p_out = slot_turn(base, 3 if more else 1, h, per)

                def v_transposes(q):
                    pe.wait_ge(a_v, h * 2 + q + 1)
                    for b in range(4):
                        last = pe.transpose(ps[:, 4 + q, blk(b)], fvT[:, blk(4 * q + b)], ident)
                    last.then_inc(a_tr, 1)

                pe.wait_ge(a_qk, h * 4 + 4)
                pe.wait_ge(a_acc, h * 16)
                pe.wait_ge(w_ready[p_v[0]], p_v[1] + 1)
                for t in range(TT):
                    if t > 0:
                        pe.wait_ge(a_t, h * 8 + t)
                    n = (t + 1) * P
                    for seg in range(0, n, HALF):
                        w = min(HALF, n - seg)
                        own = seg + w == n
                        last = product(ps[:, 2 + seg // HALF, 0:w], pair(fq2, blk(t)),
                                       pair(fk2, slice(seg, seg + w)), True, not own)
                        if own:
                            last = mm(ps[:, 2 + seg // HALF, w - P:w], identR[:, :], causalR[:, :], False, True)
                    last.then_inc(a_s, 1)
                    if t < 6:
                        half, m = t // 3, 8 * (t % 3)
                        last = job_part(half, p_v, half, m, m + 8)
                        if m == 16:
                            job_end(last, half, p_v, a_job)
                    else:
                        v_transposes(t - 6)

                def p_transposes(n):
                    g, s = steps[n]
                    if n < 2:
                        pe.wait_ge(a_vlo, h * 2 + n + 1)
                    else:
                        pe.wait_ge(a_ptlo, h * 12 + n - 1)
                    if s == 0:
                        pe.wait_ge(a_p, h * 8 + 4 * g + 4)
                    for t in range(max(4 * g, s), 4 * g + 4):
                        at = (t * (t + 1) // 2 + s) * P
                        last = pe.transpose(ps[:, 4 + n % 2, blk(t - 4 * g)], probs[:, at:at + P], ident)
                    last.then_inc(a_pt, 1)

                p_transposes(0)
                for n, (g, s) in enumerate(steps):
                    if n + 1 < len(steps):
                        p_transposes(n + 1)
                    if more:
                        j, half, m = n // 6, n // 3 % 2, 8 * (n % 3)
                        if m == 0:
                            if half == 0:
                                pe.wait_ge(w_ready[p_next[j][0]], p_next[j][1] + 1)
                            if j == 0:
                                pe.wait_ge(a_v, h * 2 + half + 1)
                            else:
                                pe.wait_ge(a_qk, h * 4 + 4 + half + 1)
                        last = job_part(half, p_next[j], half, m, m + 8)
                        if m == 16:
                            job_end(last, half, p_next[j], a_job)
                    pe.wait_ge(a_ptlo, h * 12 + n + 1)
                    c0 = max(0, s - 4 * g) * P
                    product(ps[:, 6 + g, c0:], pair(fv2[:, :, s], slice(0, DH)),
                            pair(pT2[:, n % 3], slice(c0, HALF)), s == 0, s == 4 * g + 3).then_inc(a_pv, 1)
                pe.wait_ge(a_ylo, h * 2 + 2)
                slot, turn = p_out
                pe.wait_ge(w_ready[slot], turn + 1)
                for u in range(16):
                    k, q = u // 2, u % 2
                    if u >= 4:
                        pe.wait_ge(a_acc, h * 16 + u - 3)
                    last = product(ps[:, 2 + u % 4, :], pair(w_split[:, slot], blk(k)),
                                   pair(fy2, slice(q * HALF, (q + 1) * HALF)), True, True)
                    last.then_inc(a_pj if u < 15 else w_used[slot], 1)

            with pe.Fori(0, FH - 1) as h:
                fox_head(T_FOX, h, True)
            fox_head(T_FOX, FH - 1, False)
            pe.wait_ge(a_acc, 16 * FH)
            pe.wait_ge(a_v, 2 * FH)

            def pair_stage(base, pairs, s, bread):
                def first(e, which, i, place):
                    for half in range(2):
                        n = 4 * i + 2 * e + half
                        if not (isinstance(i, int) and i == 0 and e == 0):
                            pe.wait_ge(s["ga"] if which == 0 else bread, n - 1)
                        job(2 * which + half, place, half, s["job"])

                def second(i, places):
                    pe.wait_ge(s["lo"], 4 * i + 4)
                    for slot, turn in places:
                        pe.wait_ge(w_ready[slot], turn + 1)
                    for u in range(16):
                        t, q = u // 2, u % 2
                        pe.wait_ge(s["acc"], 16 * i + max(0, u - 3))
                        for e, (slot, _) in enumerate(places):
                            last = product(ps[:, 4 + u % 4, :], pair(f2[:, e], blk(t)),
                                           pair(w_split[:, slot], slice(q * HALF, (q + 1) * HALF)), e == 0, e == 1)
                            if u == 15:
                                last.then_inc(w_used[slot], 1)
                        if u < 15:
                            last.then_inc(s["pj"], 1)

                for j in range(4):
                    first(j // 2, j % 2, 0, slot_turn(base, j))
                with pe.Fori(0, pairs - 1) as i:
                    place = [slot_turn(base + 4, j, i, PAIR_TILES) for j in range(PAIR_TILES)]
                    first(0, 0, i + 1, place[0])
                    second(i, place[1:3])
                    first(0, 1, i + 1, place[3])
                    first(1, 0, i + 1, place[4])
                    first(1, 1, i + 1, place[5])
                end = base + 4 + PAIR_TILES * (pairs - 1)
                second(pairs - 1, [slot_turn(end, e) for e in range(2)])
                pe.wait_ge(s["acc"], 16 * pairs)

            pair_stage(T_WO, KT // 2, pair_sems["o"], pair_sems["o"]["gb"])
            norm_transposes(1)
            pe.wait_ge(n_lo, 32)
            pair_stage(T_FFN, FF_PAIRS, pair_sems["f"], pair_sems["f"]["f"])

        @block.scalar
        def _(act):
            def half_of(buf, half):
                return buf[:, half * HALF:(half + 1) * HALF]

            def unit_wait(s, count, half, place):
                if half == 0:
                    act.wait_ge(s, count)
                else:
                    act.wait_ge(w_used[place[0]], place[1] + 1)

            def norm_rows(n, rows, xn, ready=None):
                for t in range(TT):
                    if ready:
                        ready(t)
                    act.activation(xn[:, t, :], rows[:, t, :], ACT.Square,
                                   accum_out=stat[:, 0, t:t + 1]).then_inc(n_sq, 1)
                act.wait_ge(n_ms, n + 1)
                act.activation(stat[:, 2, :], stat[:, 1, :], ACT.Sqrt).then_inc(n_rt, 1)

            def norm_scale(n, rows, xn):
                act.wait_ge(n_r, n + 1)
                for t in range(TT):
                    act.activation(xn[:, t, :], rows[:, t, :], ACT.Copy,
                                   scale=stat[:, 3, t:t + 1]).then_inc(n_xn, 1)

            def norm_hi(n, tmp):
                for u in range(16):
                    k, half = u // 2, u % 2
                    act.wait_ge(n_tmp, 16 * n + u + 1)
                    act.activation(half_of(hT[:, 0, k], half), tmp[:, u % 2, :], ACT.Copy).then_inc(n_hi, 1)

            act.dma_start(resid0[:, :, :], x_v).then_inc(s_x, 16)
            act.wait_ge(s_const, 96)
            act.activation(cact[:, :], cvec[:, :], ACT.Silu).then_inc(s_cact, 1)
            act.wait_ge(s_x, 16)
            norm_rows(0, resid0, macc)
            norm_scale(0, resid0, macc)
            norm_hi(0, ntmp0)
            for r in range(2):
                act.wait_ge(s_row, 2 * r + 2)
                act.dma_start(g_rows[r:r + 1, :], ntmp0[0:1, :, :].rearrange("p q c -> p (q c)")).then_inc(s_rowout, 16)
            act.wait_ge(s_rowout, 32)
            act.wait_ge(s_modT, 3)
            act.dma_start(rope[:, :, :], k_rope.rearrange("p (a s) -> p a s", a=2)).then_inc(r_const, 16)
            act.dma_start(rc[:, :], k_ret[0]).then_inc(r_const, 16)

            with act.Fori(0, RH) as h:
                place = [slot_turn(T_RET, j, h, RET_TILES) for j in range(RET_TILES)]

                def ret_wait(j, half):
                    unit_wait(r_job, h * 6 + j + 1, half, place[j])

                def v_copy(j):
                    for half in range(2):
                        ret_wait(j, half)
                        act.activation(half_of(vT[:, j - 2], half), ps[:, half, :], ACT.Copy).then_inc(r_v, 1)

                def gate(e, half):
                    ret_wait(4 + e, half)
                    act.activation(half_of(gT[:, e], half), ps[:, half, :], ACT.Silu).then_inc(r_g, 1)

                def state_hi(b):
                    act.wait_ge(r_state, h * 7 + b + 1)
                    if b >= 3:
                        act.wait_ge(r_out, h * 8 + b - 1)
                    act.activation(state2[:, b % 3, 0, :], state[:, :], ACT.Copy).then_inc(r_stahi, 1)

                def out_copy(b):
                    act.wait_ge(r_out, h * 8 + b + 1)
                    act.activation(ro[:, b, :], ps[:, 6 + b % 2, 0:DV], ACT.Copy).then_inc(r_ro, 1)
                    act.wait_ge(r_ro, h * 8 + b + 1)
                    act.activation(rsw[:, 0:DV], ro[:, b, :], ACT.Square,
                                   accum_out=rss[:, 0, b:b + 1]).then_inc(r_ss, 1)

                act.wait_ge(r_const, 32 + h * 16)
                for u in range(4):
                    j, half = u // 2, u % 2
                    ret_wait(j, half)
                    act.wait_ge(r_rot, h * 4 + u)
                    act.activation(rsw[0:P // 2, :], ps[P // 2:P, half, :], ACT.Copy)
                    act.activation(rsw[P // 2:P, :], ps[0:P // 2, half, :], ACT.Copy).then_inc(r_sw, 1)
                    act.wait_ge(r_rot, h * 4 + u + 1)
                    dst = rq2[:, 0, :] if j == 0 else kst[:, 0, 0, :]
                    act.activation(half_of(dst, half), rm[:, u % 2, :], ACT.Copy).then_inc(r_hi, 1)
                v_copy(2)
                for q in range(2):
                    act.wait_ge(r_st, h * 2 + q + 1)
                    act.activation(half_of(kst[:, 1, 0], q), rm[:, q, :], ACT.Copy).then_inc(r_sthi, 1)
                v_copy(3)
                for q in range(2):
                    act.wait_ge(r_tr, h * 6 + q + 1)
                    act.activation(kd2[:, 0, 4 * q:4 * q + 4, :],
                                   ps[:, 2 + q, :].rearrange("p (b d) -> p b d", d=P), ACT.Copy,
                                   scale=rc[:, P:P + 1]).then_inc(r_trhi, 1)
                for n in range(4):
                    e, q = n // 2, n % 2
                    act.wait_ge(r_tr, h * 6 + n + 3)
                    act.activation(rv2[:, 0, 4 * q:4 * q + 4, e * P:(e + 1) * P],
                                   ps[:, 2 + q, :].rearrange("p (b d) -> p b d", d=P), ACT.Copy).then_inc(r_trhi, 1)
                state_hi(0)
                state_hi(1)
                gate(0, 0)
                out_copy(0)
                out_copy(1)
                state_hi(2)
                state_hi(3)
                gate(0, 1)
                out_copy(2)
                out_copy(3)
                state_hi(4)
                state_hi(5)
                gate(1, 0)
                out_copy(4)
                out_copy(5)
                state_hi(6)
                out_copy(6)
                out_copy(7)
                act.wait_ge(r_ms, h + 1)
                act.activation(rss[:, 2, :], rss[:, 1, :], ACT.Sqrt).then_inc(r_rt, 1)
                gate(1, 1)
                for u in range(4):
                    e, q = u // 2, u % 2
                    act.wait_ge(r_ym, h * 4 + u + 1)
                    act.activation(half_of(kst[:, e, 0], q), rm[:, u % 2, :], ACT.Copy).then_inc(r_yhi, 1)
                act.dma_start(rc[:, :], k_ret[ds(h + 1, 1)].rearrange("o p c -> p (o c)")).then_inc(r_const, 16)

            act.wait_ge(r_const, 32 + 16 * RH)
            act.wait_ge(r_acc, 16 * RH)
            act.dma_start(ret_merge, macc[:, :, :].rearrange("p k s -> p (k s)")).then_inc(r_spill, 16)

            place = [slot_turn(T_FF, j) for j in range(3)]
            for half in range(2):
                unit_wait(g_job, 1, half, place[0])
                act.activation(half_of(fz[:, 0], half), ps[0:FH, half, :], ACT.Identity,
                               bias=bf[:, 0:1]).then_inc(g_z, 1)
            act.wait_ge(g_z, 2)
            act.activation(fz[:, 1, :], fz[:, 0, :], ACT.Abs).then_inc(g_abs, 1)
            act.wait_ge(g_abs, 1)
            act.activation(fz[:, 2, :], fz[:, 1, :], ACT.Exp, scale=-1.0).then_inc(g_exp, 1)
            act.wait_ge(g_exp, 1)
            act.activation(fz[:, 1, :], fz[:, 2, :], ACT.Ln, bias=1.0).then_inc(g_ln, 1)

            def qk_hi(n, base_count, job_count, p_of):
                j, half = n // 2, n % 2
                unit_wait(a_job, job_count + j, half, p_of[j])
                act.activation(half_of((fq2, fk2)[j][:, 0], half), ps[:, half, :], ACT.Copy,
                               scale=DH ** -0.5 if j == 0 else 1.0).then_inc(a_qkhi, 1)

            for n in range(4):
                qk_hi(n, 0, 1, place[1:])
            act.wait_ge(g_scan, 21)
            act.dma_start(negf_rows, fz[:, 2, :]).then_inc(g_store, 16)
            act.wait_ge(g_store, 16)
            act.dma_start(negf[:, :], negf_rows[0:1, :].partition_broadcast(P)).then_inc(a_nf, 16)

            def fox_head(base, h, more):
                per = FOX_TILES
                p_v = slot_turn(base, 0, h, per)
                p_next = [slot_turn(base, 1 + j, h, per) for j in range(2)]

                def v_copy(half):
                    unit_wait(a_job, h * 3 + 3, half, p_v)
                    act.activation(half_of(fvT, half), ps[:, half, :], ACT.Copy).then_inc(a_v, 1)

                def v_hi(q):
                    act.wait_ge(a_tr, h * 2 + q + 1)
                    act.activation(fv2[:, 0, 4 * q:4 * q + 4, :],
                                   ps[:, 4 + q, :].rearrange("p (b d) -> p b d", d=P), ACT.Copy).then_inc(a_vhi, 1)

                for t in range(TT):
                    act.wait_ge(a_neg, h * 8 + t + 1)
                    at = t * (t + 1) // 2 * P
                    p = probs[:, at:at + (t + 1) * P]
                    act.activation(p, p, ACT.Exp, bias=smax[:, 1, t:t + 1],
                                   accum_out=smax[:, 2, t:t + 1]).then_inc(a_e, 1)
                    if t == 2 or t == 5:
                        v_copy(t // 3)
                    if t >= 6:
                        v_hi(t - 6)
                if more:
                    act.dma_start(negf[:, :], negf_rows[ds(h + 1, 1), :].partition_broadcast(P)).then_inc(a_nf, 16)

                def y_hi(g):
                    act.wait_ge(a_pv, h * 12 + (4, 12)[g])
                    act.activation(half_of(fy2[:, 0], g), ps[:, 6 + g, :], ACT.Copy).then_inc(a_yhi, 1)

                for n, (g, s) in enumerate([(0, s) for s in range(4)] + [(1, s) for s in range(8)]):
                    act.wait_ge(a_pt, h * 12 + n + 1)
                    if n >= 3:
                        act.wait_ge(a_pv, h * 12 + n - 2)
                    c0 = max(0, s - 4 * g) * P
                    act.activation(pT2[:, n % 3, 0, c0:], ps[:, 4 + n % 2, c0:], ACT.Copy).then_inc(a_pthi, 1)
                    if more and n % 3 == 0 and n > 0:
                        qk_hi(n // 3 - 1, 0, h * 3 + 4, p_next)
                    if n == 4:
                        y_hi(0)
                if more:
                    qk_hi(3, 0, h * 3 + 4, p_next)
                y_hi(1)

            with act.Fori(0, FH - 1) as h:
                fox_head(T_FOX, h, True)
            fox_head(T_FOX, FH - 1, False)

            act.wait_ge(a_acc, 16 * FH)
            act.dma_start(grow[:, :], g_rows[0:1, :].partition_broadcast(P)).then_inc(pair_sems["o"]["grow"], 16)
            for e in range(2):
                act.dma_start(mret[:, e, :], ret_merge[:, e * S:(e + 1) * S]).then_inc(o_mret[e], 16)
            act.dma_start(resid[:, :, :], x_v).then_inc(s_x, 16)
            act.dma_start(nfrow[:, :], norm_f_w.rearrange("(o d) -> o d", o=1).partition_broadcast(P)).then_inc(s_nf, 16)

            def gates(base, i, e, order, s):
                for half in range(2):
                    n = 4 * i + 2 * e + half
                    unit_wait(s["job"], 4 * i + 2 * e + 1, half, order[0])
                    if not (isinstance(i, int) and i == 0 and e == 0):
                        act.wait_ge(s["f"], n - 1)
                    act.activation(ga[:, half, :], ps[:, half, :], ACT.Sigmoid).then_inc(s["ga"], 1)
                for half in range(2):
                    unit_wait(s["job"], 4 * i + 2 * e + 2, half, order[1])
                    act.activation(gb[:, half, :], ps[:, 2 + half, :], ACT.Sigmoid).then_inc(s["gb"], 1)
                for half in range(2):
                    hi_part(i, e, half, s)

            def silus(base, i, e, order, s):
                for half in range(2):
                    n = 4 * i + 2 * e + half
                    unit_wait(s["job"], 4 * i + 2 * e + 1, half, order[0])
                    if not (isinstance(i, int) and i == 0 and e == 0):
                        act.wait_ge(s["f"], n - 1)
                    act.activation(ga[:, half, :], ps[:, half, :], ACT.Silu).then_inc(s["ga"], 1)
                for half in range(2):
                    hi_part(i, e, half, s)

            def hi_part(i, e, half, s):
                act.wait_ge(s["f"], 4 * i + 2 * e + half + 1)
                act.activation(half_of(f2[:, e, 0], half), fin[:, half, :], ACT.Copy).then_inc(s["hi"], 1)

            def pair_act(base, pairs, s, body, before):
                first = [slot_turn(base, j) for j in range(4)]
                body(base, 0, 0, first[0:2], s)
                body(base, 0, 1, first[2:4], s)
                with act.Fori(0, pairs - 1) as i:
                    place = [slot_turn(base + 4, j, i, PAIR_TILES) for j in range(PAIR_TILES)]
                    before(i)
                    body(base, i + 1, 0, (place[0], place[3]), s)
                    body(base, i + 1, 1, (place[4], place[5]), s)

            def next_mret(i):
                for e in range(2):
                    act.dma_start(mret[:, e, :], ret_merge[:, ds((2 * i + 2 + e) * S, S)]).then_inc(o_mret[e], 16)

            pair_act(T_WO, KT // 2, pair_sems["o"], gates, next_mret)
            o = pair_sems["o"]
            act.wait_ge(w_g, KT)
            act.dma_start(grow[:, :], g_rows[1:2, :].partition_broadcast(P)).then_inc(pair_sems["f"]["grow"], 16)

            norm_rows(1, resid, macc, lambda t: act.wait_ge(o["acc"], 16 * (KT // 2 - 1) + 2 * t + 2))
            norm_scale(1, resid, macc)
            norm_hi(1, ntmp)

            pair_act(T_FFN, FF_PAIRS, pair_sems["f"], silus, lambda i: None)

            fs = pair_sems["f"]
            norm_rows(2, resid, macc, lambda t: act.wait_ge(fs["acc"], 16 * (FF_PAIRS - 1) + 2 * t + 2))
            for t in range(TT):
                act.wait_ge(f_y, t + 1)
                act.dma_start(out_v[:, t, :], resid[:, t, :]).then_inc(f_out, 16)
            act.wait_ge(f_out, 16 * TT)
            for e in range(2):
                act.wait_ge(o_mret[e], 16 * (KT // 2))

        @block.vector
        def _(dve):
            def half_of(buf, half):
                return buf[:, half * HALF:(half + 1) * HALF]

            def tt(o, a, b, op):
                return dve.tensor_tensor(o, a, b, op)

            def lo(dst_lo, value, dst_hi):
                return tt(dst_lo, value, f(dst_hi), ALU.subtract)

            def norm_mean(n):
                dve.wait_ge(n_sq, TT * (n + 1))
                dve.tensor_scalar(stat[:, 1, :], stat[:, 0, :], 1.0 / D, EPS, ALU.mult, ALU.add).then_inc(n_ms, 1)
                dve.wait_ge(n_rt, n + 1)
                dve.reciprocal(stat[:, 3, :], stat[:, 2, :]).then_inc(n_r, 1)

            def modulate(n, shift_col, tmp):
                def lo_part(u):
                    k, half = u // 2, u % 2
                    dve.wait_ge(n_hi, 16 * n + u + 1)
                    lo(half_of(hT[:, 1, k], half), tmp[:, u % 2, :], half_of(hT[:, 0, k], half)).then_inc(n_lo, 1)

                for u in range(16):
                    k = u // 2
                    dve.wait_ge(n_tr, 16 * n + u + 1)
                    if u >= 2:
                        dve.wait_ge(n_lo, 16 * n + u - 1)
                    dve.tensor_scalar(tmp[:, u % 2, :], ps[:, u % 4, :], amul[:, k:k + 1],
                                      modT[:, shift_col + k:shift_col + k + 1], ALU.mult, ALU.add).then_inc(n_tmp, 1)
                    if u > 0:
                        lo_part(u - 1)
                lo_part(15)

            dve.wait_ge(s_const, 96)
            dve.tensor_copy(identR[:, :], ident).then_inc(s_identr, 1)
            dve.tensor_copy(causalR[:, :], causal_f[:, :]).then_inc(s_identr, 1)
            dve.memset(onesf[:, :], 1.0).then_inc(s_identr, 1)
            dve.wait_ge(s_cact, 1)
            aused = [0]

            def row_copy(r):
                dve.wait_ge(s_mod, 3 + 2 * r)
                if r == 1:
                    dve.wait_ge(s_rowout, 16)
                for q in range(2):
                    dve.tensor_copy(ntmp0[0:1, q, :], ps[0:1, 4 + q, :]).then_inc(s_row, 1)

            def columns(ch):
                dve.wait_ge(s_mod, (1, 2, 4)[ch])
                dve.tensor_copy(modT[:, ch * 16:(ch + 1) * 16], ps[:, 6 + ch % 2, 0:16]).then_inc(s_modT, 1)

            for ch in range(3):
                a = ch % 2
                dve.wait_ge(s_abias, 16 * ch + 16)
                for k in range(KT):
                    n = ch * KT + k
                    dve.wait_ge(s_aload[n % 4], 16 * (n // 4) + 16)
                    if k > 0:
                        dve.wait_ge(s_aused, n)
                    ins = dve.scalar_tensor_tensor(out=ada_acc[:, a, :], in0=ada_ring[:, n % 4, :],
                                                   scalar=cact[:, k:k + 1], in1=ada_acc[:, a, :],
                                                   op0=ALU.mult, op1=ALU.add)
                    ins.then_inc(s_aused if k < KT - 1 else s_acc, 1)
                    if k == KT - 1:
                        dve.wait_ge(s_acc, ch + 1)
                        dve.tensor_copy(cvec[:, 0:1], cact[:, 0:1]).then_inc(s_aused, 1)
                if ch == 0:
                    norm_mean(0)
                    columns(0)
                    dve.wait_ge(s_modT, 1)
                    dve.scalar_tensor_tensor(out=amul[:, :], in0=modT[:, KT:2 * KT], scalar=1.0, in1=nw[:, 0, :],
                                             op0=ALU.add, op1=ALU.mult).then_inc(s_amul, 1)
                    dve.wait_ge(s_amul, 1)
                    modulate(0, 0, ntmp0)
                if ch == 1:
                    dve.wait_ge(n_lo, 16)
                    row_copy(0)
                    columns(1)
            row_copy(1)
            columns(2)

            dve.wait_ge(r_const, 32)
            dve.wait_ge(s_mzero, KT)
            with dve.Fori(0, RH) as h:
                place = [slot_turn(T_RET, j, h, RET_TILES) for j in range(RET_TILES)]
                dve.wait_ge(r_const, 32 + h * 16)

                def qk_lo(u):
                    j, half = u // 2, u % 2
                    buf = rq2 if j == 0 else kst[:, 0]
                    dve.wait_ge(r_hi, h * 4 + u + 1)
                    lo(half_of(buf[:, 1], half), rm[:, u % 2, :], half_of(buf[:, 0], half)).then_inc(r_qk, 1)

                for u in range(4):
                    half = u % 2
                    dve.wait_ge(r_sw, h * 4 + u + 1)
                    if u < 2:
                        dve.wait_ge(r_ylo, h * 4)
                    else:
                        dve.wait_ge(r_qk, h * 4 + u - 1)
                    tt(rm[:, u % 2, :], ps[:, half, :], half_of(rope[:, 0], half), ALU.mult).then_inc(r_m, 1)
                    tt(rsw[:, :], rsw[:, :], half_of(rope[:, 1], half), ALU.mult).then_inc(r_chain, 1)
                    dve.wait_ge(r_m, h * 4 + u + 1)
                    dve.wait_ge(r_chain, h * 4 + u + 1)
                    tt(rm[:, u % 2, :], rm[:, u % 2, :], rsw[:, :], ALU.add).then_inc(r_rot, 1)
                    if u > 0:
                        qk_lo(u - 1)
                qk_lo(3)

                def st_lo(q):
                    dve.wait_ge(r_sthi, h * 2 + q + 1)
                    lo(half_of(kst[:, 1, 1], q), rm[:, q, :], half_of(kst[:, 1, 0], q)).then_inc(r_stlo, 1)

                dve.wait_ge(r_qk, h * 4 + 4)
                for q in range(2):
                    dve.wait_ge(r_sc, h * 2 + q + 1)
                    tt(rm[:, q, :].rearrange("p (b t) -> p b t", t=P),
                       ps[:, 2 + q, :].rearrange("p (b t) -> p b t", t=P),
                       rc[:, 0:P].unsqueeze(1).to_broadcast([P, 4, P]), ALU.mult).then_inc(r_st, 1)
                st_lo(0)
                st_lo(1)
                for q in range(2):
                    dve.wait_ge(r_trhi, h * 6 + q + 1)
                    dve.scalar_tensor_tensor(out=kd2[:, 1, 4 * q:4 * q + 4, :].rearrange("p b d -> p (b d)"),
                                             in0=ps[:, 2 + q, :], scalar=rc[:, P:P + 1],
                                             in1=f(kd2[:, 0, 4 * q:4 * q + 4, :]).rearrange("p b d -> p (b d)"),
                                             op0=ALU.mult, op1=ALU.subtract).then_inc(r_trlo, 1)
                for n in range(4):
                    e, q = n // 2, n % 2
                    at = (slice(None), slice(4 * q, 4 * q + 4), slice(e * P, (e + 1) * P))
                    dve.wait_ge(r_trhi, h * 6 + n + 3)
                    lo(rv2[:, 1][at], ps[:, 2 + q, :].rearrange("p (b d) -> p b d", d=P),
                       rv2[:, 0][at]).then_inc(r_trlo, 1)

                def state_step(b):
                    dve.wait_ge(r_inc, h * 7 + b + 1)
                    dve.wait_ge(r_stalo, h * 7 + b)
                    if b == 0:
                        dve.tensor_copy(state[:, :], ps[:, 4, 0:DV]).then_inc(r_state, 1)
                    else:
                        dve.scalar_tensor_tensor(out=state[:, :], in0=state[:, :], scalar=rc[:, P + 3:P + 4],
                                                 in1=ps[:, 4 + b % 2, 0:DV], op0=ALU.mult,
                                                 op1=ALU.add).then_inc(r_state, 1)
                    dve.wait_ge(r_stahi, h * 7 + b + 1)
                    lo(state2[:, b % 3, 1, :], state[:, :], state2[:, b % 3, 0, :]).then_inc(r_stalo, 1)

                for b in range(7):
                    state_step(b)
                dve.wait_ge(r_ss, h * 8 + 8)
                dve.tensor_scalar(rss[:, 1, :], rss[:, 0, :], rc[:, P + 2:P + 3], EPS,
                                  ALU.mult, ALU.add).then_inc(r_ms, 1)
                dve.wait_ge(r_rt, h + 1)
                dve.reciprocal(rss[:, 3, :], rss[:, 2, :]).then_inc(r_rg, 1)
                dve.wait_ge(r_rg, h * 2 + 1)
                dve.tensor_scalar(rss[:, 3, :], rss[:, 3, :], rc[:, P + 1:P + 2], None, ALU.mult).then_inc(r_rg, 1)
                dve.wait_ge(r_rg, h * 2 + 2)
                tt(ro, ro, rss[:, 3, :].unsqueeze(2).to_broadcast([P, TT, DV]), ALU.mult).then_inc(r_ron, 1)

                def y_lo(u):
                    e, q = u // 2, u % 2
                    dve.wait_ge(r_yhi, h * 4 + u + 1)
                    lo(half_of(kst[:, e, 1], q), rm[:, u % 2, :], half_of(kst[:, e, 0], q)).then_inc(r_ylo, 1)

                dve.wait_ge(r_g, h * 4 + 4)
                for u in range(4):
                    e, q = u // 2, u % 2
                    dve.wait_ge(r_rtr, h * 4 + u + 1)
                    if u < 2:
                        dve.wait_ge(r_stlo, h * 2 + 2)
                    else:
                        dve.wait_ge(r_ylo, h * 4 + u - 1)
                    tt(rm[:, u % 2, :], ps[:, 2 + q, :], half_of(gT[:, e], q), ALU.mult).then_inc(r_ym, 1)
                    if u > 0:
                        y_lo(u - 1)
                y_lo(3)
                dve.wait_ge(r_acc, h * 16)
                for u in range(16):
                    k, q = u // 2, u % 2
                    if u < 15:
                        dve.wait_ge(r_pj, h * 15 + u + 1)
                    else:
                        dve.wait_ge(w_used[place[7][0]], place[7][1] + 1)
                    o = half_of(macc[:, k], q)
                    tt(o, ps[:, 4 + u % 4, :], o, ALU.add).then_inc(r_acc, 1)

            dve.wait_ge(g_ln, 1)
            dve.tensor_scalar(fz[:, 0, :], fz[:, 0, :], 0.0, None, ALU.min).then_inc(g_scan, 1)
            dve.wait_ge(g_scan, 1)
            tt(fz[:, 2, :], fz[:, 1, :], fz[:, 0, :], ALU.subtract)

            def scan(levels):
                for lv in levels:
                    d = 1 << lv
                    src, dst = (2, 3) if lv % 2 == 0 else (3, 2)
                    if lv == 0:
                        dve.drain()
                    else:
                        dve.wait_ge(g_scan, 2 * lv + 1)
                    dve.tensor_copy(fz[:, dst, 0:d], fz[:, src, 0:d]).then_inc(g_scan, 1)
                    tt(fz[:, dst, d:], fz[:, src, d:], fz[:, src, :S - d], ALU.add).then_inc(g_scan, 1)

            def fox_qk_lo(n, count):
                j, half = n // 2, n % 2
                buf = (fq2, fk2)[j]
                dve.wait_ge(a_qkhi, count)
                dve.scalar_tensor_tensor(out=half_of(buf[:, 1], half), in0=ps[:, half, :],
                                         scalar=DH ** -0.5 if j == 0 else 1.0, in1=f(half_of(buf[:, 0], half)),
                                         op0=ALU.mult, op1=ALU.subtract).then_inc(a_qk, 1)

            scan(range(5))
            fox_qk_lo(0, 1)
            fox_qk_lo(1, 2)
            scan(range(5, 10))
            fox_qk_lo(2, 3)
            fox_qk_lo(3, 4)

            def fox_head(base, h, more):
                def normed(t):
                    at = t * (t + 1) // 2 * P
                    dve.wait_ge(a_e, h * 8 + t + 1)
                    dve.reciprocal(smax[:, 3, t:t + 1], smax[:, 2, t:t + 1]).then_inc(a_r, 1)
                    dve.wait_ge(a_r, h * 8 + t + 1)
                    p = probs[:, at:at + (t + 1) * P]
                    dve.tensor_scalar(p, p, smax[:, 3, t:t + 1], None, ALU.mult).then_inc(a_p, 1)

                def v_lo(q):
                    dve.wait_ge(a_vhi, h * 2 + q + 1)
                    lo(fv2[:, 1, 4 * q:4 * q + 4, :], ps[:, 4 + q, :].rearrange("p (b d) -> p b d", d=P),
                       fv2[:, 0, 4 * q:4 * q + 4, :]).then_inc(a_vlo, 1)

                scores = ps[:, 2:4, :].rearrange("p b c -> p (b c)")
                dve.wait_ge(a_nf, 16 * h + 16)
                for t in range(TT):
                    n, at = (t + 1) * P, t * (t + 1) // 2 * P
                    dve.wait_ge(a_s, h * 8 + t + 1)
                    dve.tensor_copy(smax[:, 4, t:t + 1], ps[:, 2, 0:1])
                    dve.tensor_tensor_reduce(probs[:, at:at + n], scores[:, :n], negf[:, :n], 1.0, -3.0e38,
                                             ALU.add, ALU.max, smax[:, 0, t:t + 1]).then_inc(a_t, 1)
                    dve.wait_ge(a_t, h * 8 + t + 1)
                    dve.tensor_scalar(smax[:, 1, t:t + 1], smax[:, 0, t:t + 1], -1.0, None,
                                      ALU.mult).then_inc(a_neg, 1)
                    if t > 0:
                        normed(t - 1)
                v_lo(0)
                normed(TT - 1)
                v_lo(1)

                def y_lo(g):
                    dve.wait_ge(a_yhi, h * 2 + g + 1)
                    lo(half_of(fy2[:, 1], g), ps[:, 6 + g, :], half_of(fy2[:, 0], g)).then_inc(a_ylo, 1)

                for n, (g, s) in enumerate([(0, s) for s in range(4)] + [(1, s) for s in range(8)]):
                    c0 = max(0, s - 4 * g) * P
                    dve.wait_ge(a_pthi, h * 12 + n + 1)
                    lo(pT2[:, n % 3, 1, c0:], ps[:, 4 + n % 2, c0:], pT2[:, n % 3, 0, c0:]).then_inc(a_ptlo, 1)
                    if more and n % 3 == 0 and n > 0:
                        fox_qk_lo(n // 3 - 1, h * 4 + 4 + n // 3)
                    if n == 4:
                        y_lo(0)
                if more:
                    fox_qk_lo(3, h * 4 + 8)
                y_lo(1)
                slot, turn = slot_turn(base, 3 if more else 1, h, FOX_TILES)
                for u in range(16):
                    k, q = u // 2, u % 2
                    if u < 15:
                        dve.wait_ge(a_pj, h * 15 + u + 1)
                    else:
                        dve.wait_ge(w_used[slot], turn + 1)
                    o = half_of(macc[:, k], q)
                    tt(o, ps[:, 2 + u % 4, :], o, ALU.add).then_inc(a_acc, 1)

            dve.wait_ge(s_mzero, 2 * KT)
            with dve.Fori(0, FH - 1) as h:
                fox_head(T_FOX, h, True)
            fox_head(T_FOX, FH - 1, False)

            def merge(i, e, s):
                k = 2 * i + e
                dve.wait_ge(o_mret[e], 16 * i + 16)
                for half in range(2):
                    n = 4 * i + 2 * e + half
                    dve.wait_ge(s["ga"], n + 1)
                    tt(ga[:, half, :], ga[:, half, :], half_of(mret[:, e], half), ALU.mult).then_inc(s["gm"], 1)
                for half in range(2):
                    n = 4 * i + 2 * e + half
                    dve.wait_ge(s["gb"], n + 1)
                    m = macc_half(k, half)
                    tt(gb[:, half, :], gb[:, half, :], m, ALU.mult).then_inc(s["gbm"], 1)
                    dve.wait_ge(s["gbm"], n + 1)
                    dve.wait_ge(s["gm"], n + 1)
                    if not (isinstance(i, int) and i == 0 and e == 0):
                        dve.wait_ge(s["lo"], n - 1)
                    tt(fin[:, half, :], ga[:, half, :], gb[:, half, :], ALU.add).then_inc(s["f"], 1)
                for half in range(2):
                    lo_part(i, e, half, s)

            def macc_half(k, half):
                flat = macc[:, :, :].rearrange("p k s -> p (k s)")
                return flat[:, ds(k * S + half * HALF, HALF)]

            def swiglu(i, e, s, place):
                for half in range(2):
                    n = 4 * i + 2 * e + half
                    if half == 0:
                        dve.wait_ge(s["job"], 4 * i + 2 * e + 2)
                    else:
                        dve.wait_ge(w_used[place[0]], place[1] + 1)
                    dve.wait_ge(s["ga"], n + 1)
                    if not (isinstance(i, int) and i == 0 and e == 0):
                        dve.wait_ge(s["lo"], n - 1)
                    tt(fin[:, half, :], ps[:, 2 + half, :], ga[:, half, :], ALU.mult).then_inc(s["f"], 1)
                for half in range(2):
                    lo_part(i, e, half, s)

            def lo_part(i, e, half, s):
                dve.wait_ge(s["hi"], 4 * i + 2 * e + half + 1)
                lo(half_of(f2[:, e, 1], half), fin[:, half, :], half_of(f2[:, e, 0], half)).then_inc(s["lo"], 1)

            def add_second(i, s, place):
                for u in range(16):
                    t, q = u // 2, u % 2
                    if u < 15:
                        dve.wait_ge(s["pj"], 15 * i + u + 1)
                    else:
                        dve.wait_ge(w_used[place[0]], place[1] + 1)
                    o = half_of(resid[:, t], q)
                    tt(o, ps[:, 4 + u % 4, :], o, ALU.add).then_inc(s["acc"], 1)

            def pair_dve(base, pairs, s, body):
                first = [slot_turn(base, j) for j in range(4)]
                body(0, 0, s, first[1])
                body(0, 1, s, first[3])
                with dve.Fori(0, pairs - 1) as i:
                    place = [slot_turn(base + 4, j, i, PAIR_TILES) for j in range(PAIR_TILES)]
                    add_second(i, s, place[2])
                    body(i + 1, 0, s, place[3])
                    body(i + 1, 1, s, place[5])
                end = base + 4 + PAIR_TILES * (pairs - 1)
                add_second(pairs - 1, s, slot_turn(end, 1))

            dve.wait_ge(s_x, 32)
            pair_dve(T_WO, KT // 2, pair_sems["o"], lambda i, e, s, place: merge(i, e, s))
            norm_mean(1)
            dve.scalar_tensor_tensor(out=amul[:, :], in0=modT[:, 4 * KT:5 * KT], scalar=1.0, in1=nw[:, 1, :],
                                     op0=ALU.add, op1=ALU.mult).then_inc(s_amul, 1)
            dve.wait_ge(s_amul, 2)
            modulate(1, 3 * KT, ntmp)
            pair_dve(T_FFN, FF_PAIRS, pair_sems["f"], swiglu)

            norm_mean(2)
            dve.wait_ge(n_r, 3)
            dve.wait_ge(s_nf, 16)
            for t in range(TT):
                dve.scalar_tensor_tensor(out=resid[:, t, :], in0=resid[:, t, :], scalar=stat[:, 3, t:t + 1],
                                         in1=nfrow[:, :], op0=ALU.mult, op1=ALU.mult).then_inc(f_y, 1)


_INS = ["x", "c", "ada_w", "ada_b", "norm1_w", "w_in", "b_f", "ret_proj", "fox_proj", "w_out",
        "norm2_w", "w_gate", "w_up", "w_down", "norm_f_w"]


def kernel(**inputs):
    import concourse.bacc as bacc
    from concourse.bass_utils import run_bass_kernel_spmd

    nc = bacc.Bacc("TRN2", target_bir_lowering=False, num_devices=1)
    arrays = {n: np.ascontiguousarray(inputs[n]) for n in _INS}
    for n in ("c", "norm1_w", "norm2_w"):
        arrays[n] = np.ascontiguousarray(arrays[n].reshape(KT, P).T)
    arrays["b_f"] = arrays["b_f"].reshape(FH, 1)
    arrays.update({"k_" + n: a for n, a in host_constants().items()})
    feeds, args = {}, []
    for name, a in arrays.items():
        feeds[f"in_{name}"] = a
        args.append(nc.dram_tensor(f"in_{name}", a.shape, mybir.dt.from_np(a.dtype), kind="ExternalInput").ap())
    out = nc.dram_tensor("out_0", (1, S, D), F32, kind="ExternalOutput").ap()
    hybrid_block(nc, *args, out)
    return run_bass_kernel_spmd(nc, [feeds], core_ids=[0]).results[0]["out_0"]
```

```python
import concourse.bass as bass
from concourse import mybir
from contextlib import ExitStack
import numpy as np

F32 = mybir.dt.float32
F32R = mybir.dt.float32r
ALU = mybir.AluOpType
ACT = mybir.ActivationFunctionType

P = 128
D = 1024
S = 1024
KT = D // P
TT = S // P
HALF = 512
RH, DK, DV, CHUNK = 4, 128, 256, 64
FH, DH = 8, 128
D_FF = (((8 * D + 2) // 3 + 255) // 256) * 256
EPS = 1e-6
RET_QK, RET_V, FOX_W = RH * DK, RH * DV, FH * DH
(O_RQ, O_RK, O_RV, O_RG, O_FQ, O_FK, O_FV, O_FF, O_GR, O_GF) = np.cumsum(
    [0, RET_QK, RET_QK, RET_V, RET_V, FOX_W, FOX_W, FOX_W, FH, D]).tolist()
NEG = -(2.0 ** 100)
FF_PAIRS = D_FF // (2 * P)

RET_TILES = 8
T_RET = 0
T_FF = T_RET + RET_TILES * RH
T_FOX = T_FF + 3
FOX_TILES = 4
T_WO = T_FOX + FOX_TILES * (FH - 1) + 2
SLOTS = 4
PAIR_TILES = 6
T_FFN = T_WO + PAIR_TILES * (D // (2 * P))

RC = P + 4


def host_constants():
    half = DK // 2
    freqs = np.float32(10000.0) ** (-np.arange(half, dtype=np.float32) / np.float32(half))
    ang = np.arange(S, dtype=np.float32)[None, :] * freqs.astype(np.float32)[:, None]
    cos, sin = np.cos(ang), np.sin(ang)
    rope = np.stack([np.concatenate([cos, cos]), np.concatenate([-sin, sin])], 1)
    ident = np.eye(P)
    s, t = np.arange(P)[:, None], np.arange(P)[None, :]
    causal = np.where(t <= s, 0.0, NEG)
    ret = np.zeros((RH + 1, P, RC))
    for h in range(RH):
        lg = np.log(1.0 - 2.0 ** (-5.0 - h))
        seen = (s // CHUNK) <= (t // CHUNK)
        ret[h, :, :P] = np.where(seen, np.exp(lg * (np.abs(t - s) - t)), 0.0) * DK ** -0.5
        i = np.arange(P)
        ret[h, :, P] = np.exp(lg * (P - i)) * DK ** -0.5
        ret[h, :, P + 1] = np.exp(lg * i)
        ret[h, :, P + 2] = np.exp(2 * lg * i) / DV
        ret[h, :, P + 3] = np.exp(lg * P)
    mats = np.concatenate([ident, causal], 1)
    return {k: np.ascontiguousarray(v, dtype=np.float32)
            for k, v in {"mats": mats, "rope": rope.reshape(P, 2 * S), "ret": ret}.items()}


def hybrid_block(nc, x, c, ada_w, ada_b, norm1_w, w_in, b_f, ret_proj, fox_proj, w_out, norm2_w,
                 w_gate, w_up, w_down, norm_f_w, k_mats, k_rope, k_ret, out):
    ds = bass.ds
    x_v = x[0].rearrange("(n p) d -> p n d", p=P)
    out_v = out[0].rearrange("(n p) d -> p n d", p=P)
    ada_v = ada_w[0]
    w_in_v = w_in[0].rearrange("(k p) c -> p k c", p=P)
    gate_v = w_gate[0].rearrange("(k p) c -> p k c", p=P)
    up_v = w_up[0].rearrange("(k p) c -> p k c", p=P)
    retp, foxp, wout, wdown = ret_proj[0], fox_proj[0], w_out[0], w_down[0]

    g_rows = nc.dram_tensor("g_rows", (2, D), F32).ap()
    negf_rows = nc.dram_tensor("negf_rows", (FH, S), F32).ap()
    ret_merge = nc.dram_tensor("ret_merge", (P, KT * S), F32).ap()

    ctx = ExitStack()
    with ctx:
        def sb(name, shape, dt=F32, stack=ctx):
            return stack.enter_context(nc.sbuf_tensor("b_" + name, shape, dt))

        def sem(name):
            return ctx.enter_context(nc.semaphore(name))

        def f(ap):
            return ap.bitcast(F32)

        ps = ctx.enter_context(nc.psum_tensor("ps", [P, 8, HALF], F32))

        hT = sb("hT", [P, 2, KT, S], F32R)
        w_split = sb("w_split", [P, SLOTS, 2, 1024], F32R)
        w_stage = sb("w_stage", [P, 2, 1024])
        macc = sb("macc", [P, KT, S])
        ident_f = sb("ident_f", [P, P])
        ident = ident_f[:, :]
        causal_f = macc[:, 0, 0:P]
        identR = sb("identR", [P, P], F32R)
        causalR = sb("causalR", [P, P], F32R)
        modT = sb("modT", [P, 48])
        nw = sb("nw", [P, 2, KT])
        amul = sb("amul", [P, KT])
        begun = sb("begun", [P, 3])
        spare = sb("spare", [P, 1])
        cvec = sb("cvec", [P, KT])
        cact = sb("cact", [P, KT])
        bf = sb("bf", [FH, 1])
        stat = sb("stat", [P, 4, TT])

        ones = sb("ones", [P, 1])
        flat = macc[:, :, :].rearrange("p k s -> p (k s)")
        ada_acc2 = flat[:, 0:4096].rearrange("p (a c) -> p a c", a=2)
        ada_ring2 = flat[:, 4096:8192].rearrange("p (a c) -> p a c", a=2)
        grows = flat[0:1, 4096:6144]

        st = ExitStack()
        ntmp0 = sb("ntmp0", [P, 2, HALF], F32, st)
        ada_acc = sb("ada_acc", [P, 2048], F32, st)
        resid0 = sb("resid0", [P, TT, D], F32, st)
        ada_ring = sb("ada_ring", [P, 4, 2048], F32, st)
        ada_early = [resid0[:, 5:7, :].rearrange("p a c -> p (a c)"), ada_ring[:, 0, :], ada_ring[:, 3, :]]
        st.close()

        st = ExitStack()
        rq2 = sb("rq2", [P, 2, S], F32R, st)
        kst = sb("kst", [P, 2, 2, S], F32R, st)
        vt_ro = sb("vt_ro", [P, 2048], F32, st)
        rv2 = sb("rv2", [P, 2, TT, DV], F32R, st)
        kd2 = sb("kd2", [P, 2, TT, DK], F32R, st)
        rm = sb("rm", [P, 2, HALF], F32, st)
        rsw = sb("rsw", [P, HALF], F32, st)
        junk, state = rsw[:, 0:DV], rsw[:, DV:2 * DV]
        state2 = sb("state2", [P, 3, 2, DV], F32R, st)
        gT = sb("gT", [P, 2, S], F32, st)
        rope = sb("rope", [P, 2, S], F32, st)
        rc = sb("rc", [P, RC], F32, st)
        rss = sb("rss", [P, 4, TT], F32, st)
        st.close()
        vT = vt_ro[:, :].rearrange("p (e s) -> p e s", e=2)
        ro = vt_ro[:, :].rearrange("p (b e) -> p b e", e=DV)

        st = ExitStack()
        fq2 = sb("fq2", [P, 2, S], F32R, st)
        fk2 = sb("fk2", [P, 2, S], F32R, st)
        fv2 = sb("fv2", [P, 2, TT, DH], F32R, st)
        fvT = sb("fvT", [P, S], F32, st)
        probs = sb("probs", [P, TT * (TT + 1) // 2 * P], F32, st)
        pT2 = sb("pT2", [P, 3, 2, HALF], F32R, st)
        fy2 = sb("fy2", [P, 2, S], F32R, st)
        negf = sb("negf", [P, S], F32, st)
        smax = sb("smax", [P, 5, TT], F32, st)
        st.close()
        fz = probs[0:FH, 0:4 * S].rearrange("p (a s) -> p a s", a=4)

        st = ExitStack()
        resid = sb("resid", [P, TT, D], F32, st)
        ntmp = sb("ntmp", [P, 4, HALF], F32, st)
        f2 = sb("f2", [P, 2, 2, S], F32R, st)
        ga = sb("ga", [P, 2, HALF], F32, st)
        gb = sb("gb", [P, 2, HALF], F32, st)
        fin = sb("fin", [P, 2, HALF], F32, st)
        mret = sb("mret", [P, 2, S], F32, st)
        grow = sb("grow", [P, D], F32, st)
        nfrow = sb("nfrow", [P, D], F32, st)
        st.close()

        s_const = sem("s_const")
        s_identr = sem("s_identr")
        w_loaded = [sem(f"w_loaded{i}") for i in range(2)]
        w_hi = [sem(f"w_hi{i}") for i in range(SLOTS)]
        w_ready = [sem(f"w_ready{i}") for i in range(SLOTS)]
        w_used = [sem(f"w_used{i}") for i in range(SLOTS)]
        w_g = sem("w_g")
        s_x = sem("s_x")
        s_cact = sem("s_cact")
        s_aload = [sem(f"s_aload{i}") for i in range(4)]
        s_aused = sem("s_aused")
        s_azero = sem("s_azero")
        s_abias = sem("s_abias")
        s_early = [sem(f"s_early{i}") for i in range(3)]
        s_aload2 = [sem(f"s_aload2{i}") for i in range(2)]
        s_mod = sem("s_mod")
        s_modT = sem("s_modT")
        s_row = sem("s_row")
        s_rowout = sem("s_rowout")
        s_amul = sem("s_amul")
        n_sq, n_ms, n_rt, n_r, n_xn = (sem(f"n_{k}") for k in ("sq", "ms", "rt", "r", "xn"))
        n_tr, n_hi, n_lo = (sem(f"n_{k}") for k in ("tr", "hi", "lo"))
        n_tmp = [sem("n_tmp_dve"), sem("n_tmp_act")]
        s_mzero = sem("s_mzero")
        r_const = sem("r_const")
        r_job, r_sw, r_m, r_chain, r_rot, r_hi, r_qk = (
            sem(f"r_{k}") for k in ("job", "sw", "m", "chain", "rot", "hi", "qk"))
        r_v, r_g, r_sc, r_st, r_sthi, r_stlo = (sem(f"r_{k}") for k in ("v", "g", "sc", "st", "sthi", "stlo"))
        r_tr, r_trhi, r_trlo = (sem(f"r_{k}") for k in ("tr", "trhi", "trlo"))
        r_inc, r_state, r_stahi, r_stalo = (sem(f"r_{k}") for k in ("inc", "state", "stahi", "stalo"))
        r_out, r_ro, r_ss, r_ms, r_rt, r_rg, r_ron = (
            sem(f"r_{k}") for k in ("out", "ro", "ss", "ms", "rt", "rg", "ron"))
        r_rtr, r_ym, r_yhi, r_ylo, r_pj, r_acc = (sem(f"r_{k}") for k in ("rtr", "ym", "yhi", "ylo", "pj", "acc"))
        r_spill = sem("r_spill")
        g_job, g_z, g_abs, g_exp, g_ln, g_scan, g_store = (
            sem(f"g_{k}") for k in ("job", "z", "abs", "exp", "ln", "scan", "store"))
        a_job, a_qkhi, a_qk, a_v, a_tr, a_vhi, a_vlo = (
            sem(f"a_{k}") for k in ("job", "qkhi", "qk", "v", "tr", "vhi", "vlo"))
        a_nf, a_s, a_t, a_neg, a_e, a_r, a_p = (sem(f"a_{k}") for k in ("nf", "s", "t", "neg", "e", "r", "p"))
        a_pt, a_pthi, a_ptlo, a_pv, a_yhi, a_ylo, a_pj, a_acc = (
            sem(f"a_{k}") for k in ("pt", "pthi", "ptlo", "pv", "yhi", "ylo", "pj", "acc"))
        pair_sems = {k: {n: sem(f"{k}_{n}") for n in (
            "job", "ga", "gm", "gb", "gbm", "f", "hi", "lo", "pj", "acc", "grow")} for k in "of"}
        o_mret = [sem(f"o_mret{i}") for i in range(2)]
        s_nf = sem("s_nf")
        f_y = sem("f_y")
        f_out = sem("f_out")

        block = ctx.enter_context(nc.Block())

        def slot_turn(base, j, it=0, per=0):
            n = base + j
            return n % SLOTS, it * (per // SLOTS) + n // SLOTS

        def may_follow(turn):
            return not isinstance(turn, int) or turn > 0

        def norm_unit(u):
            return u // KT, u % KT

        def later_pairs(eng, base, pairs, later):
            if pairs - 1 < 6:
                for p in range(1, pairs):
                    later(p, base + 4 + PAIR_TILES * (p - 1), 0)
                return
            assert (pairs - 1) % 2 == 0
            with eng.Fori(0, (pairs - 1) // 2) as i:
                for q in range(2):
                    later(2 * i + 1 + q, base + 4, PAIR_TILES * q, i, 2 * PAIR_TILES)

        @block.sync
        def _(sp):
            sp.dma_start(ident, k_mats[:, 0:P]).then_inc(s_const, 16)
            sp.dma_start(causal_f, k_mats[:, P:2 * P]).then_inc(s_const, 16)
            sp.dma_start(cvec[:, :], c).then_inc(s_const, 16)
            sp.dma_start(nw[:, 0, :], norm1_w).then_inc(s_const, 16)
            sp.dma_start(nw[:, 1, :], norm2_w).then_inc(s_const, 16)
            sp.dma_start(bf[:, :], b_f).then_inc(s_const, 16)
            sp.wait_ge(s_azero, 1)
            sp.dma_start(ada_acc[0:1, :], ada_b[0:1, 0:2048]).then_inc(s_abias, 16)
            for k in range(KT):
                if k >= 4:
                    sp.wait_ge(s_aused, k - 3)
                sp.dma_start(ada_ring[:, k % 4, :], ada_v[k * P:(k + 1) * P, 0:2048]).then_inc(s_aload[k % 4], 16)

            EARLY = len(ada_early)

            def later_ada(n):
                ch, k = 1 + n // KT, n % KT
                if k == 0:
                    sp.wait_ge(s_azero, 1 + ch)
                    sp.dma_start(ada_acc2[0:1, ch - 1, :],
                                 ada_b[0:1, ch * 2048:(ch + 1) * 2048]).then_inc(s_abias, 16)
                if n < EARLY:
                    return
                if n >= EARLY + 2:
                    sp.wait_ge(s_aused, KT + n - 1)
                sp.dma_start(ada_ring2[:, n % 2, :],
                             ada_v[k * P:(k + 1) * P, ch * 2048:(ch + 1) * 2048]).then_inc(s_aload2[n % 2], 16)

            def load(src, base, j, it=0, per=0, cols=True):
                n = base + j
                slot, turn = slot_turn(base, j - 2, it, per)
                if not isinstance(turn, int) or n >= 2:
                    sp.wait_ge(w_ready[slot], turn + 1)
                dst = w_stage[:, n % 2, :]
                if cols:
                    dst = dst.rearrange("p (k c) -> p k c", c=P)
                sp.dma_start(dst, src).then_inc(w_loaded[n % 2], 16)

            def retention_load(h, j):
                if j < 6:
                    s0 = (O_RQ + h * DK, O_RK + h * DK, O_RV + h * DV, O_RV + h * DV + P,
                          O_RG + h * DV, O_RG + h * DV + P)[j]
                    load(w_in_v[:, :, ds(s0, P)], T_RET, j, h, RET_TILES)
                else:
                    load(retp[ds(h * DV + (j - 6) * P, P), :], T_RET, j, h, RET_TILES, cols=False)

            for j in range(2):
                retention_load(0, j)
            sp.wait_ge(n_xn, TT)
            sp.wait_ge(s_aused, KT)
            for n in range(EARLY):
                sp.dma_start(ada_early[n], ada_v[n * P:(n + 1) * P, 2048:4096]).then_inc(s_early[n], 16)
            for j in range(2, 6):
                retention_load(0, j)
            for n in range(2 * KT):
                later_ada(n)
                if n in (4, 6):
                    retention_load(0, 6 + (n - 4) // 2)
            with sp.Fori(0, RH - 1) as i:
                for j in range(RET_TILES):
                    retention_load(i + 1, j)

            for j, s0 in enumerate((O_FF, O_FQ, O_FK)):
                load(w_in_v[:, :, s0:s0 + P], T_FF, j)
            with sp.Fori(0, FH - 1) as h:
                for j, s0 in enumerate((O_FV + h * DH, O_FQ + (h + 1) * DH, O_FK + (h + 1) * DH)):
                    load(w_in_v[:, :, ds(s0, P)], T_FOX, j, h, FOX_TILES)
                load(foxp[ds(h * DH, P), :], T_FOX, 3, h, FOX_TILES, cols=False)
            last = T_FOX + FOX_TILES * (FH - 1)
            load(w_in_v[:, :, O_FV + (FH - 1) * DH:O_FV + FH * DH], last, 0)
            load(foxp[(FH - 1) * DH:FH * DH, :], last, 1, cols=False)

            def pair_loads(base, pairs, a_of, b_of, w2):
                for j, (m, e) in enumerate(((a_of, 0), (b_of, 0), (a_of, 1), (b_of, 1))):
                    load(m(e), base, j)
                def later(p, base, j0, it=0, per=0):
                    load(a_of(2 * p), base, j0, it, per)
                    for e in range(2):
                        load(w2[ds((2 * p - 2 + e) * P, P), :], base, j0 + 1 + e, it, per, cols=False)
                    load(b_of(2 * p), base, j0 + 3, it, per)
                    load(a_of(2 * p + 1), base, j0 + 4, it, per)
                    load(b_of(2 * p + 1), base, j0 + 5, it, per)

                later_pairs(sp, base, pairs, later)
                end = base + 4 + PAIR_TILES * (pairs - 1)
                for e in range(2):
                    r = (2 * (pairs - 1) + e) * P
                    load(w2[r:r + P, :], end, e, cols=False)

            pair_loads(T_WO, KT // 2, lambda t: w_in_v[:, :, ds(O_GR + t * P, P)],
                       lambda t: w_in_v[:, :, ds(O_GF + t * P, P)], wout)
            pair_loads(T_FFN, FF_PAIRS, lambda t: gate_v[:, :, ds(t * P, P)],
                       lambda t: up_v[:, :, ds(t * P, P)], wdown)
            for t in range(TT):
                sp.wait_ge(f_y, t + 1)
                sp.dma_start(out_v[:, t, :], resid[:, t, :]).then_inc(f_out, 16)
            sp.wait_ge(f_out, 16 * TT)
            sp.wait_ge(s_rowout, 16)
            sp.wait_ge(r_spill, 16)
            sp.wait_ge(g_store, 16)

        @block.gpsimd
        def _(pool):
            pool.memset(ada_acc[:, :], 0.0).then_inc(s_azero, 1)

            def split(base, j, it=0, per=0, scaled=False):
                slot, turn = slot_turn(base, j, it, per)
                n = base + j
                src = w_stage[:, n % 2, :]
                hi, lo = w_split[:, slot, 0, :], w_split[:, slot, 1, :]
                pool.wait_ge(w_loaded[n % 2], 16 * (it * (per // 2) + n // 2) + 16)
                if scaled:
                    pool.tensor_tensor(src, src, grow[:, :], ALU.mult).then_inc(w_g, 1)
                return slot, turn, src, hi, lo

            def finish(base, j, part):
                slot, turn, src, hi, lo = part
                if may_follow(turn):
                    pool.wait_ge(w_used[slot], turn)
                pool.tensor_tensor(spare[0:1, :], src[0:1, 0:1], src[0:1, 0:1], ALU.add)
                pool.tensor_scalar(hi, src, 1.0, None, ALU.mult).then_inc(w_hi[slot], 1)
                pool.wait_ge(w_hi[slot], turn + 1)
                pool.tensor_tensor(lo, src, f(hi), ALU.subtract).then_inc(w_ready[slot], 1)

            def tile(base, j, it=0, per=0):
                finish(base, j, split(base, j, it, per))

            def scaled_tile(base, j, count, it=0, per=0):
                part = split(base, j, it, per, scaled=True)
                pool.wait_ge(w_g, count)
                finish(base, j, part)

            for j in range(4):
                tile(T_RET, j)
            pool.wait_ge(n_tr, 16)
            for ch in range(2):
                pool.memset(ada_acc2[:, ch, :], 0.0).then_inc(s_azero, 1)
            for j in range(4, RET_TILES):
                tile(T_RET, j)
            with pool.Fori(0, RH - 1) as i:
                for j in range(RET_TILES):
                    tile(T_RET, j, i + 1, RET_TILES)
            for j in range(3):
                tile(T_FF, j)
            pool.wait_ge(r_spill, 16)
            for k in range(KT):
                pool.memset(macc[:, k, :], 0.0).then_inc(s_mzero, 1)
            with pool.Fori(0, FH - 1) as h:
                for j in range(FOX_TILES):
                    tile(T_FOX, j, h, FOX_TILES)
            for j in range(2):
                tile(T_FOX + FOX_TILES * (FH - 1), j)

            def pair_splits(base, pairs, sems, scaled_before):
                for j in range(4):
                    tile(base, j)
                pool.wait_ge(sems["grow"], 16)

                def later(p, base, j0, it=0, per=0):
                    tile(base, j0, it, per)
                    for e in range(2):
                        scaled_tile(base, j0 + 1 + e, scaled_before + 2 * p - 1 + e, it, per)
                    for j in range(3, 6):
                        tile(base, j0 + j, it, per)

                later_pairs(pool, base, pairs, later)
                end = base + 4 + PAIR_TILES * (pairs - 1)
                for e in range(2):
                    scaled_tile(end, e, scaled_before + 2 * (pairs - 1) + e + 1)

            pair_splits(T_WO, KT // 2, pair_sems["o"], 0)
            pair_splits(T_FFN, FF_PAIRS, pair_sems["f"], KT)

        @block.tensor
        def _(pe):
            def mm(o, l, r, start, stop):
                return pe.matmul(o, l, r, start=start, stop=stop)

            def product(o, l, r, start, stop):
                mm(o, l[0], r[0], start, False)
                mm(o, l[0], r[1], False, False)
                return mm(o, l[1], r[0], False, stop)

            def pair(buf, cols):
                return buf[:, 0, cols], buf[:, 1, cols]

            def blk(t):
                return slice(t * P, (t + 1) * P)

            def job_part(bank, place, half, m0, m1):
                for m in range(m0, m1):
                    k, which = m // 3, m % 3
                    w = w_split[:, place[0], int(which == 2), blk(k)]
                    a = hT[:, int(which == 1), k, half * HALF:(half + 1) * HALF]
                    last = mm(ps[:, bank, :], w, a, m == 0, m == 23)
                return last

            def job_end(last, half, place, s):
                last.then_inc(s if half == 0 else w_used[place[0]], 1)

            def job(bank, place, half, s):
                if half == 0:
                    pe.wait_ge(w_ready[place[0]], place[1] + 1)
                job_end(job_part(bank, place, half, 0, 24), half, place, s)

            def norm_transposes(n, units):
                for u in units:
                    half, k = norm_unit(u)
                    if k == 0:
                        pe.wait_ge(n_xn, TT * n + 4 * half + 4)
                    if u >= 4:
                        pe.wait_ge(n_tmp[u % 2], 8 * n + u // 2 - 1)
                    for b in range(4):
                        last = pe.transpose(ps[:, 4 + u % 4, blk(b)], macc[:, 4 * half + b, blk(k)], ident)
                    last.then_inc(n_tr, 1)

            def first_job(n, place, s, between=None):
                pe.wait_ge(w_ready[place[0]], place[1] + 1)
                for k in range(KT):
                    norm_transposes(n, [KT + k])
                    pe.wait_ge(n_lo, 16 * n + k + 1)
                    last = job_part(0, place, 0, 3 * k, 3 * k + 3)
                job_end(last, 0, place, s)
                if between:
                    between()
                pe.wait_ge(n_lo, 16 * n + 16)
                job(1, place, 1, s)

            pe.wait_ge(s_const, 96)
            pe.wait_ge(s_identr, 3)
            pe.wait_ge(s_aused, KT)
            for b in range(16):
                last = mm(ps[:, 0, b:b + 1], ada_acc[:, blk(b)], ones[:, :], True, True)
            last.then_inc(s_mod, 1)
            norm_transposes(0, range(KT))

            def later_vectors():
                pe.wait_ge(s_aused, 3 * KT)
                pe.wait_ge(r_state, 7)
                pe.wait_ge(r_ro, 8)
                pe.wait_ge(r_g, 4)
                for b in range(KT, 3 * KT):
                    mm(ps[:, 0, b:b + 1], ada_acc2[:, b // 16, blk(b % 16)], ones[:, :], True, True)
                for r, at in enumerate((0, D)):
                    for q in range(2):
                        last = mm(ps[0:1, 4 + 2 * r + q, :], ones[:, :],
                                  ada_acc2[:, r, at + q * HALF:at + (q + 1) * HALF], True, True)
                last.then_inc(s_mod, 1)

            BEGUN = 16

            def rest_begun(place, s):
                job_end(job_part(0, place, 0, BEGUN, 24), 0, place, s)

            def ret_head(h, first):
                place = [slot_turn(T_RET, j, h, RET_TILES) for j in range(RET_TILES)]
                following = slot_turn(T_RET, RET_TILES, h, RET_TILES)

                def ret_job(j, half):
                    u = 2 * j + half
                    if u < 2:
                        pe.wait_ge(r_g, h * 4)
                    elif u < 6:
                        pe.wait_ge(r_m, h * 4 + u - 1)
                    elif u < 10:
                        pe.wait_ge(r_v, h * 4 + u - 5)
                    else:
                        pe.wait_ge(r_g, h * 4 + u - 9)
                    job(u % 2, place[j], half, r_job)

                if first:
                    pe.wait_ge(s_modT, 1)
                    first_job(0, place[0], r_job, lambda: job(2, place[1], 0, r_job))
                else:
                    rest_begun(place[0], r_job)
                    ret_job(0, 1)
                for j in (1, 2):
                    if not (first and j == 1):
                        ret_job(j, 0)
                    ret_job(j, 1)
                pe.wait_ge(r_qk, h * 4 + 4)
                pe.wait_ge(r_ym, h * 4)
                for q in range(2):
                    for b in range(4):
                        t = 4 * q + b
                        last = product(ps[:, 2 + q, blk(b)], pair(kst[:, 0], blk(t)), pair(rq2, blk(t)), True, True)
                    last.then_inc(r_sc, 1)
                ret_job(3, 0)
                ret_job(3, 1)
                for q in range(2):
                    pe.wait_ge(r_st, h * 2 + q + 1)
                    for b in range(4):
                        t = 4 * q + b
                        mm(ps[:, 2 + q, blk(b)], kst[:, 0, 0, blk(t)], identR[:, :], True, False)
                        last = mm(ps[:, 2 + q, blk(b)], kst[:, 0, 1, blk(t)], identR[:, :], False, True)
                    last.then_inc(r_tr, 1)
                pe.wait_ge(r_v, h * 4 + 4)
                for n in range(4):
                    e, q = n // 2, n % 2
                    if n == 0:
                        pe.wait_ge(w_ready[place[4][0]], place[4][1] + 1)
                    job_part(0, place[4], 0, (0, 4, 6, 8)[n], (4, 6, 8, 10)[n])
                    pe.wait_ge(r_trlo, h * 6 + n + 1)
                    for b in range(4):
                        last = pe.transpose(ps[:, 2 + q, blk(b)], vT[:, e, blk(4 * q + b)], ident)
                    last.then_inc(r_tr, 1)

                def added(b):
                    if b == 0:
                        pe.wait_ge(r_trlo, h * 6 + 6)
                        pe.wait_ge(r_acc, h * 16)
                    if b >= 2:
                        pe.wait_ge(r_state, h * 7 + b - 1)
                    product(ps[:, 4 + b % 2, 0:DV], pair(kd2[:, :, b], slice(0, DK)),
                            pair(rv2[:, :, b], slice(0, DV)), True, True).then_inc(r_inc, 1)

                def output(b):
                    if b == 0:
                        pe.wait_ge(r_stlo, h * 2 + 2)
                    if b >= 2:
                        pe.wait_ge(r_ro, h * 8 + b - 1)
                    o = ps[:, 6 + b % 2, 0:DV]
                    last = product(o, pair(kst[:, 1], blk(b)), pair(rv2[:, :, b], slice(0, DV)), True, b == 0)
                    if b > 0:
                        pe.wait_ge(r_stalo, h * 7 + b)
                        last = product(o, pair(rq2, blk(b)), pair(state2[:, (b - 1) % 3], slice(0, DV)), False, True)
                    last.then_inc(r_out, 1)

                job_part(0, place[4], 0, 10, 15)
                added(0)
                added(1)
                job_end(job_part(0, place[4], 0, 15, 24), 0, place[4], r_job)
                output(0)
                output(1)
                added(2)
                added(3)
                ret_job(4, 1)
                output(2)
                output(3)
                added(4)
                added(5)
                pe.wait_ge(w_ready[place[5][0]], place[5][1] + 1)
                pe.wait_ge(r_g, h * 4 + 1)
                job_part(0, place[5], 0, 0, 16)
                output(4)
                output(5)
                added(6)
                job_end(job_part(0, place[5], 0, 16, 24), 0, place[5], r_job)
                output(6)
                output(7)
                pe.wait_ge(r_g, h * 4 + 2)
                job_part(1, place[5], 1, 0, 18)
                for u in range(4):
                    q, e = u // 2, u % 2
                    if e == 0:
                        pe.wait_ge(r_ron, h * 2 + q + 1)
                    if u >= 2:
                        pe.wait_ge(r_ym, h * 4 + u - 1)
                    for b in range(4):
                        last = pe.transpose(ps[:, 2 + e, blk(b)], ro[:, 4 * q + b, blk(e)], ident)
                    last.then_inc(r_rtr, 1)
                    if u == 1:
                        job_end(job_part(1, place[5], 1, 18, 24), 1, place[5], None)
                if first:
                    later_vectors()
                pe.wait_ge(w_ready[following[0]], following[1] + 1)
                pe.wait_ge(r_g, h * 4 + 3)
                if first:
                    pe.wait_ge(s_modT, 2)
                job_part(0, following, 0, 0, BEGUN)
                for slot, turn in place[6:]:
                    pe.wait_ge(w_ready[slot], turn + 1)
                for u in range(16):
                    q, k = u // KT, u % KT
                    if k == 0:
                        pe.wait_ge(r_ylo, h * 4 + 2 * q + 2)
                    if first and u == 0:
                        pe.wait_ge(s_row, 4)
                    if u >= 4:
                        pe.wait_ge(r_acc, h * 16 + u - 3)
                    for e in range(2):
                        slot = place[6 + e][0]
                        last = product(ps[:, 4 + u % 4, :], pair(w_split[:, slot], blk(k)),
                                       pair(kst[:, e], slice(q * HALF, (q + 1) * HALF)), e == 0, e == 1)
                        if u == 15:
                            last.then_inc(w_used[slot], 1)
                    if u < 15:
                        last.then_inc(r_pj, 1)

            ret_head(0, True)
            with pe.Fori(0, RH - 1) as i:
                ret_head(i + 1, False)

            place = [slot_turn(T_FF, j) for j in range(3)]
            pe.wait_ge(r_g, 4 * RH)
            rest_begun(place[0], g_job)
            job(1, place[0], 1, g_job)
            for j in (1, 2):
                for half in range(2):
                    if j == 1:
                        pe.wait_ge(g_z, half + 1)
                    else:
                        pe.wait_ge(a_qk, half + 1)
                    job(half, place[j], half, a_job)
            pe.wait_ge(r_ym, 4 * RH)
            pe.wait_ge(r_acc, 16 * RH)

            steps = [(0, s) for s in range(4)] + [(1, s) for s in range(8)]

            def fox_head(base, h, more):
                per = FOX_TILES
                p_v = slot_turn(base, 0, h, per)
                p_next = [slot_turn(base, 1 + j, h, per) for j in range(2)]
                p_out = slot_turn(base, 3 if more else 1, h, per)

                def v_transposes(q):
                    pe.wait_ge(a_v, h * 2 + q + 1)
                    for b in range(4):
                        last = pe.transpose(ps[:, 6 + q, blk(b)], fvT[:, blk(4 * q + b)], ident)
                    last.then_inc(a_tr, 1)

                p_wo = slot_turn(T_WO, 0)

                def next_part(m0, m1):
                    if not more:
                        for m in range(m0, m1):
                            half, at = m // 24, m % 24
                            if at == 0 and half == 0:
                                pe.wait_ge(w_ready[p_wo[0]], p_wo[1] + 1)
                            if at == 0:
                                pe.wait_ge(a_v, h * 2 + half + 1)
                            last = job_part(half, p_wo, half, at, at + 1)
                            if at == 23:
                                job_end(last, half, p_wo, pair_sems["o"]["job"])
                        return
                    for m in range(m0, m1):
                        j, half, at = m // 48, m // 24 % 2, m % 24
                        if at == 0:
                            if half == 0:
                                pe.wait_ge(w_ready[p_next[j][0]], p_next[j][1] + 1)
                            if j == 0:
                                pe.wait_ge(a_v, h * 2 + half + 1)
                            else:
                                pe.wait_ge(a_qk, h * 4 + 4 + half + 1)
                        last = job_part(half, p_next[j], half, at, at + 1)
                        if at == 23:
                            job_end(last, half, p_next[j], a_job)

                pe.wait_ge(a_qk, h * 4 + 4)
                pe.wait_ge(w_ready[p_v[0]], p_v[1] + 1)
                for t in range(TT):
                    if t < 6:
                        half, m = t // 3, 8 * (t % 3)
                        last = job_part(half, p_v, half, m, m + 8)
                        if m == 16:
                            job_end(last, half, p_v, a_job)
                    else:
                        v_transposes(t - 6)
                        next_part(8 * (t - 6), 8 * (t - 5))
                    if t == 0:
                        pe.wait_ge(a_acc, h * 16 + 1)
                    else:
                        pe.wait_ge(a_t, h * 8 + t)
                    n = (t + 1) * P
                    for seg in range(0, n, HALF):
                        w = min(HALF, n - seg)
                        own = seg + w == n
                        last = product(ps[:, 2 + seg // HALF, 0:w], pair(fq2, blk(t)),
                                       pair(fk2, slice(seg, seg + w)), True, not own)
                        if own:
                            last = mm(ps[:, 2 + seg // HALF, w - P:w], identR[:, :], causalR[:, :], False, True)
                    last.then_inc(a_s, 1)

                def p_transposes(n):
                    g, s = steps[n]
                    if n >= 2:
                        pe.wait_ge(a_ptlo, h * 12 + n - 1)
                    if s == 0:
                        pe.wait_ge(a_p, h * 8 + 4 * g + 4)
                    for t in range(max(4 * g, s), 4 * g + 4):
                        at = (t * (t + 1) // 2 + s) * P
                        last = pe.transpose(ps[:, 4 + n % 2, blk(t - 4 * g)], probs[:, at:at + P], ident)
                    last.then_inc(a_pt, 1)

                if more:
                    fill = [16, 32] + [36 + 6 * n for n in range(len(steps) - 1)]
                else:
                    fill = [16, 26] + [28 + 2 * n for n in range(len(steps) - 1)]
                p_transposes(0)
                for n, (g, s) in enumerate(steps):
                    if n + 1 < len(steps):
                        p_transposes(n + 1)
                    next_part(fill[n], fill[n + 1])
                    pe.wait_ge(a_ptlo, h * 12 + n + 1)
                    if s == 0:
                        pe.wait_ge(a_vlo, h * 2 + g + 1)
                    c0 = max(0, s - 4 * g) * P
                    product(ps[:, 6 + g, c0:], pair(fv2[:, :, s], slice(0, DH)),
                            pair(pT2[:, n % 3], slice(c0, HALF)), s == 0, s == 4 * g + 3).then_inc(a_pv, 1)
                slot, turn = p_out
                pe.wait_ge(w_ready[slot], turn + 1)
                for u in range(16):
                    q, k = u // KT, u % KT
                    if k == 0:
                        pe.wait_ge(a_ylo, h * 2 + q + 1)
                    if u >= 4:
                        pe.wait_ge(a_acc, h * 16 + u - 2)
                    last = product(ps[:, 2 + u % 4, :], pair(w_split[:, slot], blk(k)),
                                   pair(fy2, slice(q * HALF, (q + 1) * HALF)), True, True)
                    last.then_inc(a_pj if u < 15 else w_used[slot], 1)

            with pe.Fori(0, FH - 1) as h:
                fox_head(T_FOX, h, True)
            fox_head(T_FOX, FH - 1, False)
            pe.wait_ge(a_acc, 16 * FH + 1)
            pe.wait_ge(a_v, 2 * FH)

            def pair_stage(base, pairs, s, bread, norm=None):
                def first(e, which, i, place):
                    for half in range(2):
                        n = 4 * i + 2 * e + half
                        if not (isinstance(i, int) and i == 0 and e == 0):
                            pe.wait_ge(s["ga"] if which == 0 else bread, n - 1)
                        job(2 * which + half, place, half, s["job"])

                def second(i, places):
                    def part(u, e):
                        t, q = u // 2, u % 2
                        slot = places[e][0]
                        last = product(ps[:, 4 + u % 4, :], pair(f2[:, e], blk(t)),
                                       pair(w_split[:, slot], slice(q * HALF, (q + 1) * HALF)), e == 0, e == 1)
                        if u == 15:
                            last.then_inc(w_used[slot], 1)
                        elif e == 1:
                            last.then_inc(s["pj"], 1)

                    pe.wait_ge(s["lo"], 4 * i + 2)
                    pe.wait_ge(w_ready[places[0][0]], places[0][1] + 1)
                    pe.wait_ge(s["acc"], 16 * i + 1)
                    for u in range(4):
                        part(u, 0)
                    pe.wait_ge(s["lo"], 4 * i + 4)
                    pe.wait_ge(w_ready[places[1][0]], places[1][1] + 1)
                    for u in range(4):
                        part(u, 1)
                    for u in range(4, 16):
                        pe.wait_ge(s["acc"], 16 * i + u - 2)
                        part(u, 0)
                        part(u, 1)

                for j in range(4):
                    if norm is not None and j < 2:
                        if j == 0:
                            norm_transposes(norm, range(KT))
                            first_job(norm, slot_turn(base, 0), s["job"],
                                      lambda: job(2, slot_turn(base, 1), 0, s["job"]))
                        else:
                            job(3, slot_turn(base, 1), 1, s["job"])
                    elif norm is not None or j > 0:
                        first(j // 2, j % 2, 0, slot_turn(base, j))

                def later(p, base, j0, it=0, per=0):
                    place = [slot_turn(base, j0 + j, it, per) for j in range(PAIR_TILES)]
                    first(0, 0, p, place[0])
                    second(p - 1, place[1:3])
                    first(0, 1, p, place[3])
                    first(1, 0, p, place[4])
                    first(1, 1, p, place[5])

                later_pairs(pe, base, pairs, later)
                end = base + 4 + PAIR_TILES * (pairs - 1)
                second(pairs - 1, [slot_turn(end, e) for e in range(2)])
                pe.wait_ge(s["acc"], 16 * pairs + 1)

            pair_stage(T_WO, KT // 2, pair_sems["o"], pair_sems["o"]["gb"])
            pair_stage(T_FFN, FF_PAIRS, pair_sems["f"], pair_sems["f"]["f"], norm=1)

        @block.scalar
        def _(act):
            def half_of(buf, half):
                return buf[:, half * HALF:(half + 1) * HALF]

            def unit_wait(s, count, half, place):
                if half == 0:
                    act.wait_ge(s, count)
                else:
                    act.wait_ge(w_used[place[0]], place[1] + 1)

            def norm_rows(n, rows, xn, ready=None, scale=True):
                for t in range(TT + 2):
                    if t < TT:
                        if ready:
                            ready(t)
                        act.activation(xn[:, t, :], rows[:, t, :], ACT.Square,
                                       accum_out=stat[:, 0, t:t + 1]).then_inc(n_sq, 1)
                    if 0 <= t - 1 < TT:
                        act.wait_ge(n_ms, n * TT + t)
                        act.activation(stat[:, 2, t - 1:t], stat[:, 1, t - 1:t], ACT.Sqrt).then_inc(n_rt, 1)
                    if t >= 2 and scale:
                        act.wait_ge(n_r, n * TT + t - 1)
                        act.activation(xn[:, t - 2, :], rows[:, t - 2, :], ACT.Copy,
                                       scale=stat[:, 3, t - 2:t - 1]).then_inc(n_xn, 1)

            def norm_hi(n, shift_col, tmp):
                depth = tmp.shape[1]
                act.wait_ge(s_amul, n + 1)
                for u in range(16):
                    half, k = norm_unit(u)
                    if u % 2 == 1:
                        act.wait_ge(n_tr, 16 * n + u + 1)
                        if u >= depth:
                            act.wait_ge(n_lo, 16 * n + u - depth + 1)
                        act.activation(tmp[:, u % depth, :], ps[:, 4 + u % 4, :], ACT.Identity,
                                       scale=amul[:, k:k + 1],
                                       bias=modT[:, shift_col + k:shift_col + k + 1]).then_inc(n_tmp[1], 1)
                    act.wait_ge(n_tmp[u % 2], 8 * n + u // 2 + 1)
                    act.activation(half_of(hT[:, 0, k], half), tmp[:, u % depth, :], ACT.Copy).then_inc(n_hi, 1)

            act.dma_start(resid0[:, :, :], x_v).then_inc(s_x, 16)
            act.dma_start(rope[:, :, :], k_rope.rearrange("p (a s) -> p a s", a=2)).then_inc(r_const, 16)
            act.dma_start(rc[:, :], k_ret[0]).then_inc(r_const, 16)
            act.wait_ge(s_const, 96)
            act.activation(cact[:, :], cvec[:, :], ACT.Silu).then_inc(s_cact, 1)
            act.wait_ge(s_x, 16)
            act.wait_ge(s_identr, 2)
            norm_rows(0, resid0, macc)
            norm_hi(0, 0, ntmp0)
            def ret_head(h, first):
                place = [slot_turn(T_RET, j, h, RET_TILES) for j in range(RET_TILES)]

                def ret_wait(j, half):
                    unit_wait(r_job, h * 6 + j + 1, half, place[j])

                def v_copy(j):
                    for half in range(2):
                        ret_wait(j, half)
                        act.activation(half_of(vT[:, j - 2], half), ps[:, half, :], ACT.Copy).then_inc(r_v, 1)

                def gate(e, half):
                    ret_wait(4 + e, half)
                    act.activation(half_of(gT[:, e], half), ps[:, half, :], ACT.Silu).then_inc(r_g, 1)

                def state_hi(b):
                    act.wait_ge(r_state, h * 7 + b + 1)
                    if b >= 3:
                        act.wait_ge(r_out, h * 8 + b - 1)
                    act.activation(state2[:, b % 3, 0, :], state, ACT.Copy).then_inc(r_stahi, 1)

                def out_copy(b):
                    act.wait_ge(r_out, h * 8 + b + 1)
                    act.activation(ro[:, b, :], ps[:, 6 + b % 2, 0:DV], ACT.Copy).then_inc(r_ro, 1)
                    act.wait_ge(r_ro, h * 8 + b + 1)
                    act.activation(junk, ro[:, b, :], ACT.Square,
                                   accum_out=rss[:, 0, b:b + 1]).then_inc(r_ss, 1)

                act.wait_ge(r_const, 32 + h * 16)
                for u in range(4):
                    j, half = u // 2, u % 2
                    ret_wait(j, half)
                    act.wait_ge(r_rot, h * 4 + u)
                    bank = 2 if first and u == 2 else half
                    act.activation(rsw[0:P // 2, :], ps[P // 2:P, bank, :], ACT.Copy)
                    act.activation(rsw[P // 2:P, :], ps[0:P // 2, bank, :], ACT.Copy).then_inc(r_sw, 1)
                    act.wait_ge(r_rot, h * 4 + u + 1)
                    dst = rq2[:, 0, :] if j == 0 else kst[:, 0, 0, :]
                    act.activation(half_of(dst, half), rm[:, u % 2, :], ACT.Copy).then_inc(r_hi, 1)
                v_copy(2)
                for q in range(2):
                    act.wait_ge(r_st, h * 2 + q + 1)
                    act.activation(half_of(kst[:, 1, 0], q), rm[:, q, :], ACT.Copy).then_inc(r_sthi, 1)
                v_copy(3)
                for q in range(2):
                    act.wait_ge(r_tr, h * 6 + q + 1)
                    act.activation(kd2[:, 0, 4 * q:4 * q + 4, :],
                                   ps[:, 2 + q, :].rearrange("p (b d) -> p b d", d=P), ACT.Copy,
                                   scale=rc[:, P:P + 1]).then_inc(r_trhi, 1)
                for n in range(4):
                    e, q = n // 2, n % 2
                    act.wait_ge(r_tr, h * 6 + n + 3)
                    act.activation(rv2[:, 0, 4 * q:4 * q + 4, e * P:(e + 1) * P],
                                   ps[:, 2 + q, :].rearrange("p (b d) -> p b d", d=P), ACT.Copy).then_inc(r_trhi, 1)
                state_hi(0)
                state_hi(1)
                gate(0, 0)
                out_copy(0)
                out_copy(1)
                state_hi(2)
                state_hi(3)
                gate(0, 1)
                out_copy(2)
                out_copy(3)
                state_hi(4)
                state_hi(5)
                out_copy(4)
                out_copy(5)
                state_hi(6)
                gate(1, 0)
                out_copy(6)
                out_copy(7)
                act.wait_ge(r_ms, h + 1)
                act.activation(rss[:, 2, :], rss[:, 1, :], ACT.Sqrt).then_inc(r_rt, 1)
                for u in range(4):
                    q, e = u // 2, u % 2
                    if u == 2:
                        gate(1, 1)
                    act.wait_ge(r_ym, h * 4 + u + 1)
                    act.activation(half_of(kst[:, e, 0], q), rm[:, u % 2, :], ACT.Copy).then_inc(r_yhi, 1)
                if first:
                    act.wait_ge(s_row, 4)
                    act.dma_start(g_rows.rearrange("(o a) b -> o (a b)", o=1), grows).then_inc(s_rowout, 16)
                act.dma_start(rc[:, :], k_ret[ds(h + 1, 1)].rearrange("o p c -> p (o c)")).then_inc(r_const, 16)

            act.wait_ge(n_lo, 16)
            ret_head(0, True)
            with act.Fori(0, RH - 1) as i:
                ret_head(i + 1, False)
            act.wait_ge(r_const, 32 + 16 * RH)
            act.wait_ge(r_acc, 16 * RH)
            act.dma_start(ret_merge, macc[:, :, :].rearrange("p k s -> p (k s)")).then_inc(r_spill, 16)

            place = [slot_turn(T_FF, j) for j in range(3)]
            for half in range(2):
                unit_wait(g_job, 1, half, place[0])
                act.activation(half_of(fz[:, 0], half), ps[0:FH, half, :], ACT.Identity,
                               bias=bf[:, 0:1]).then_inc(g_z, 1)
            act.wait_ge(g_z, 2)
            act.activation(fz[:, 1, :], fz[:, 0, :], ACT.Abs).then_inc(g_abs, 1)
            act.wait_ge(g_abs, 1)
            act.activation(fz[:, 2, :], fz[:, 1, :], ACT.Exp, scale=-1.0).then_inc(g_exp, 1)
            act.wait_ge(g_exp, 1)
            act.activation(fz[:, 1, :], fz[:, 2, :], ACT.Ln, bias=1.0).then_inc(g_ln, 1)

            def qk_hi(n, base_count, job_count, p_of):
                j, half = n // 2, n % 2
                unit_wait(a_job, job_count + j, half, p_of[j])
                act.activation(half_of((fq2, fk2)[j][:, 0], half), ps[:, half, :], ACT.Copy,
                               scale=DH ** -0.5 if j == 0 else 1.0).then_inc(a_qkhi, 1)

            for n in range(4):
                qk_hi(n, 0, 1, place[1:])
            act.wait_ge(g_scan, 21)
            act.dma_start(negf_rows, fz[:, 2, :]).then_inc(g_store, 16)
            act.wait_ge(g_store, 16)
            act.dma_start(negf[:, :], negf_rows[0:1, :].partition_broadcast(P)).then_inc(a_nf, 16)

            def fox_head(base, h, more):
                per = FOX_TILES
                p_v = slot_turn(base, 0, h, per)
                p_next = [slot_turn(base, 1 + j, h, per) for j in range(2)]

                def v_copy(half):
                    unit_wait(a_job, h * 3 + 3, half, p_v)
                    act.activation(half_of(fvT, half), ps[:, half, :], ACT.Copy).then_inc(a_v, 1)

                def v_hi(q):
                    act.wait_ge(a_tr, h * 2 + q + 1)
                    act.activation(fv2[:, 0, 4 * q:4 * q + 4, :],
                                   ps[:, 6 + q, :].rearrange("p (b d) -> p b d", d=P), ACT.Copy).then_inc(a_vhi, 1)

                for t in range(TT):
                    if t >= 6:
                        v_hi(t - 6)
                    act.wait_ge(a_neg, h * 8 + t + 1)
                    at = t * (t + 1) // 2 * P
                    p = probs[:, at:at + (t + 1) * P]
                    act.activation(p, p, ACT.Exp, bias=smax[:, 1, t:t + 1],
                                   accum_out=smax[:, 2, t:t + 1]).then_inc(a_e, 1)
                    if t == 2 or t == 5:
                        v_copy(t // 3)
                if more:
                    act.dma_start(negf[:, :], negf_rows[ds(h + 1, 1), :].partition_broadcast(P)).then_inc(a_nf, 16)

                def y_hi(g):
                    act.wait_ge(a_pv, h * 12 + (4, 12)[g])
                    act.activation(half_of(fy2[:, 0], g), ps[:, 6 + g, :], ACT.Copy).then_inc(a_yhi, 1)

                for n, (g, s) in enumerate([(0, s) for s in range(4)] + [(1, s) for s in range(8)]):
                    act.wait_ge(a_pt, h * 12 + n + 1)
                    if n >= 3:
                        act.wait_ge(a_pv, h * 12 + n - 2)
                    c0 = max(0, s - 4 * g) * P
                    act.activation(pT2[:, n % 3, 0, c0:], ps[:, 4 + n % 2, c0:], ACT.Copy).then_inc(a_pthi, 1)
                    if more and n % 3 == 0 and n > 0:
                        qk_hi(n // 3 - 1, 0, h * 3 + 4, p_next)
                    if n == 4:
                        y_hi(0)
                if more:
                    qk_hi(3, 0, h * 3 + 4, p_next)
                y_hi(1)

            with act.Fori(0, FH - 1) as h:
                fox_head(T_FOX, h, True)
            fox_head(T_FOX, FH - 1, False)

            act.wait_ge(a_acc, 16 * FH + 1)
            act.dma_start(grow[:, :], g_rows[0:1, :].partition_broadcast(P)).then_inc(pair_sems["o"]["grow"], 16)
            for e in range(2):
                act.dma_start(mret[:, e, :], ret_merge[:, e * S:(e + 1) * S]).then_inc(o_mret[e], 16)
            act.dma_start(resid[:, :, :], x_v).then_inc(s_x, 16)
            act.dma_start(nfrow[:, :], norm_f_w.rearrange("(o d) -> o d", o=1).partition_broadcast(P)).then_inc(s_nf, 16)

            def gates(base, i, e, order, s):
                for half in range(2):
                    n = 4 * i + 2 * e + half
                    unit_wait(s["job"], 4 * i + 2 * e + 1, half, order[0])
                    if not (isinstance(i, int) and i == 0 and e == 0):
                        act.wait_ge(s["f"], n - 1)
                    act.activation(ga[:, half, :], ps[:, half, :], ACT.Sigmoid).then_inc(s["ga"], 1)
                for half in range(2):
                    unit_wait(s["job"], 4 * i + 2 * e + 2, half, order[1])
                    act.activation(gb[:, half, :], ps[:, 2 + half, :], ACT.Sigmoid).then_inc(s["gb"], 1)
                for half in range(2):
                    hi_part(i, e, half, s)

            def silus(base, i, e, order, s):
                for half in range(2):
                    n = 4 * i + 2 * e + half
                    unit_wait(s["job"], 4 * i + 2 * e + 1, half, order[0])
                    if not (isinstance(i, int) and i == 0 and e == 0):
                        act.wait_ge(s["f"], n - 1)
                    act.activation(ga[:, half, :], ps[:, half, :], ACT.Silu).then_inc(s["ga"], 1)
                for half in range(2):
                    hi_part(i, e, half, s)

            def hi_part(i, e, half, s):
                act.wait_ge(s["f"], 4 * i + 2 * e + half + 1)
                act.activation(half_of(f2[:, e, 0], half), fin[:, half, :], ACT.Copy).then_inc(s["hi"], 1)

            def pair_act(base, pairs, s, body, before):
                first = [slot_turn(base, j) for j in range(4)]
                body(base, 0, 0, first[0:2], s)
                body(base, 0, 1, first[2:4], s)

                def later(p, base, j0, it=0, per=0):
                    place = [slot_turn(base, j0 + j, it, per) for j in range(PAIR_TILES)]
                    before(p - 1)
                    body(base, p, 0, (place[0], place[3]), s)
                    body(base, p, 1, (place[4], place[5]), s)

                later_pairs(act, base, pairs, later)

            def next_mret(i):
                for e in range(2):
                    act.dma_start(mret[:, e, :], ret_merge[:, ds((2 * i + 2 + e) * S, S)]).then_inc(o_mret[e], 16)

            pair_act(T_WO, KT // 2, pair_sems["o"], gates, next_mret)
            o = pair_sems["o"]
            act.wait_ge(w_g, KT)
            act.dma_start(grow[:, :], g_rows[1:2, :].partition_broadcast(P)).then_inc(pair_sems["f"]["grow"], 16)

            norm_rows(1, resid, macc, lambda t: act.wait_ge(o["acc"], 16 * (KT // 2 - 1) + 2 * t + 3))
            norm_hi(1, 3 * KT, ntmp)

            pair_act(T_FFN, FF_PAIRS, pair_sems["f"], silus, lambda i: None)

            fs = pair_sems["f"]
            norm_rows(2, resid, macc, lambda t: act.wait_ge(fs["acc"], 16 * (FF_PAIRS - 1) + 2 * t + 3),
                      scale=False)
            for e in range(2):
                act.wait_ge(o_mret[e], 16 * (KT // 2))

        @block.vector
        def _(dve):
            def half_of(buf, half):
                return buf[:, half * HALF:(half + 1) * HALF]

            def tt(o, a, b, op):
                return dve.tensor_tensor(o, a, b, op)

            def lo(dst_lo, value, dst_hi):
                return tt(dst_lo, value, f(dst_hi), ALU.subtract)

            def mean(n, t):
                dve.wait_ge(n_sq, TT * n + t + 1)
                dve.tensor_scalar(stat[:, 1, t:t + 1], stat[:, 0, t:t + 1], 1.0 / D, EPS,
                                  ALU.mult, ALU.add).then_inc(n_ms, 1)

            def inverse(n, t):
                dve.wait_ge(n_rt, TT * n + t + 1)
                dve.reciprocal(stat[:, 3, t:t + 1], stat[:, 2, t:t + 1]).then_inc(n_r, 1)

            def norm_steps(n, t, final=None):
                if 0 <= t - 1 < TT:
                    mean(n, t - 1)
                if 0 <= t - 2 < TT:
                    inverse(n, t - 2)
                if final and 0 <= t - 3 < TT:
                    final(t - 3)

            def modulate(n, shift_col, tmp):
                depth = tmp.shape[1]

                def lo_part(u):
                    half, k = norm_unit(u)
                    dve.wait_ge(n_hi, 16 * n + u + 1)
                    lo(half_of(hT[:, 1, k], half), tmp[:, u % depth, :], half_of(hT[:, 0, k], half)).then_inc(n_lo, 1)

                for u in range(16):
                    half, k = norm_unit(u)
                    if u % 2 == 0:
                        dve.wait_ge(n_tr, 16 * n + u + 1)
                        if u >= depth:
                            dve.wait_ge(n_lo, 16 * n + u - depth + 1)
                        dve.tensor_scalar(tmp[:, u % depth, :], ps[:, 4 + u % 4, :], amul[:, k:k + 1],
                                          modT[:, shift_col + k:shift_col + k + 1],
                                          ALU.mult, ALU.add).then_inc(n_tmp[0], 1)
                    if u >= depth // 2:
                        lo_part(u - depth // 2)
                for u in range(16 - depth // 2, 16):
                    lo_part(u)

            dve.wait_ge(s_const, 96)
            dve.tensor_copy(identR[:, :], ident).then_inc(s_identr, 1)
            dve.tensor_copy(causalR[:, :], causal_f).then_inc(s_identr, 1)
            dve.memset(ones[:, :], 1.0).then_inc(s_identr, 1)
            dve.wait_ge(s_cact, 1)

            dve.wait_ge(s_abias, 16)
            for k in range(KT):
                dve.wait_ge(s_aload[k % 4], 16 * (k // 4) + 16)
                if k > 0:
                    dve.wait_ge(s_aused, k)
                dve.scalar_tensor_tensor(out=ada_acc[:, :], in0=ada_ring[:, k % 4, :], scalar=cact[:, k:k + 1],
                                         in1=ada_acc[:, :], op0=ALU.mult, op1=ALU.add).then_inc(s_aused, 1)
                norm_steps(0, k + 1)
            for t in range(TT + 1, TT + 2):
                norm_steps(0, t)
            dve.wait_ge(s_mod, 1)
            dve.tensor_copy(modT[:, 0:16], ps[:, 0, 0:16]).then_inc(s_modT, 1)
            dve.wait_ge(s_modT, 1)
            dve.scalar_tensor_tensor(out=amul[:, :], in0=modT[:, KT:2 * KT], scalar=1.0, in1=nw[:, 0, :],
                                     op0=ALU.add, op1=ALU.mult).then_inc(s_amul, 1)
            dve.wait_ge(s_amul, 1)
            modulate(0, 0, ntmp0)

            def ada_sums(first, units):
                for n in units if first else ():
                    ch, k = n // KT, n % KT
                    if k == 0:
                        dve.wait_ge(s_abias, 16 * ch + 32)
                    early = len(ada_early)
                    if n < early:
                        dve.wait_ge(s_early[n], 16)
                        src = ada_early[n]
                    else:
                        dve.wait_ge(s_aload2[n % 2], 16 * ((n - early) // 2) + 16)
                        src = ada_ring2[:, n % 2, :]
                    dve.wait_ge(s_aused, KT + n)
                    dve.scalar_tensor_tensor(out=ada_acc2[:, ch, :], in0=src,
                                             scalar=cact[:, k:k + 1], in1=ada_acc2[:, ch, :],
                                             op0=ALU.mult, op1=ALU.add).then_inc(s_aused, 1)

            def ret_head(h, first):
                place = [slot_turn(T_RET, j, h, RET_TILES) for j in range(RET_TILES)]
                dve.wait_ge(r_const, 32 + h * 16)

                def qk_lo(u):
                    j, half = u // 2, u % 2
                    buf = rq2 if j == 0 else kst[:, 0]
                    dve.wait_ge(r_hi, h * 4 + u + 1)
                    lo(half_of(buf[:, 1], half), rm[:, u % 2, :], half_of(buf[:, 0], half)).then_inc(r_qk, 1)

                for u in range(4):
                    half = u % 2
                    dve.wait_ge(r_sw, h * 4 + u + 1)
                    if u < 2:
                        dve.wait_ge(r_ylo, h * 4)
                    else:
                        dve.wait_ge(r_qk, h * 4 + u - 1)
                    bank = 2 if first and u == 2 else half
                    tt(rm[:, u % 2, :], ps[:, bank, :], half_of(rope[:, 0], half), ALU.mult).then_inc(r_m, 1)
                    tt(rsw[:, :], rsw[:, :], half_of(rope[:, 1], half), ALU.mult).then_inc(r_chain, 1)
                    dve.wait_ge(r_m, h * 4 + u + 1)
                    dve.wait_ge(r_chain, h * 4 + u + 1)
                    tt(rm[:, u % 2, :], rm[:, u % 2, :], rsw[:, :], ALU.add).then_inc(r_rot, 1)
                    if u > 0:
                        qk_lo(u - 1)
                    ada_sums(first, [u])
                qk_lo(3)

                def st_lo(q):
                    dve.wait_ge(r_sthi, h * 2 + q + 1)
                    lo(half_of(kst[:, 1, 1], q), rm[:, q, :], half_of(kst[:, 1, 0], q)).then_inc(r_stlo, 1)

                ada_sums(first, [4, 5])
                dve.wait_ge(r_qk, h * 4 + 4)
                for q in range(2):
                    dve.wait_ge(r_sc, h * 2 + q + 1)
                    tt(rm[:, q, :].rearrange("p (b t) -> p b t", t=P),
                       ps[:, 2 + q, :].rearrange("p (b t) -> p b t", t=P),
                       rc[:, 0:P].unsqueeze(1).to_broadcast([P, 4, P]), ALU.mult).then_inc(r_st, 1)
                st_lo(0)
                st_lo(1)
                ada_sums(first, [6, 7, 8])
                for q in range(2):
                    dve.wait_ge(r_trhi, h * 6 + q + 1)
                    dve.scalar_tensor_tensor(out=kd2[:, 1, 4 * q:4 * q + 4, :].rearrange("p b d -> p (b d)"),
                                             in0=ps[:, 2 + q, :], scalar=rc[:, P:P + 1],
                                             in1=f(kd2[:, 0, 4 * q:4 * q + 4, :]).rearrange("p b d -> p (b d)"),
                                             op0=ALU.mult, op1=ALU.subtract).then_inc(r_trlo, 1)
                for n in range(4):
                    e, q = n // 2, n % 2
                    at = (slice(None), slice(4 * q, 4 * q + 4), slice(e * P, (e + 1) * P))
                    dve.wait_ge(r_trhi, h * 6 + n + 3)
                    lo(rv2[:, 1][at], ps[:, 2 + q, :].rearrange("p (b d) -> p b d", d=P),
                       rv2[:, 0][at]).then_inc(r_trlo, 1)

                def state_step(b):
                    dve.wait_ge(r_inc, h * 7 + b + 1)
                    dve.wait_ge(r_stalo, h * 7 + b)
                    if b == 0:
                        dve.tensor_copy(state, ps[:, 4, 0:DV]).then_inc(r_state, 1)
                    else:
                        dve.scalar_tensor_tensor(out=state, in0=state, scalar=rc[:, P + 3:P + 4],
                                                 in1=ps[:, 4 + b % 2, 0:DV], op0=ALU.mult,
                                                 op1=ALU.add).then_inc(r_state, 1)
                    dve.wait_ge(r_stahi, h * 7 + b + 1)
                    lo(state2[:, b % 3, 1, :], state, state2[:, b % 3, 0, :]).then_inc(r_stalo, 1)

                for b in range(7):
                    state_step(b)
                    ada_sums(first, [9 + b] if b < 6 else ())
                dve.wait_ge(r_ss, h * 8 + 8)
                dve.tensor_scalar(rss[:, 1, :], rss[:, 0, :], rc[:, P + 2:P + 3], EPS,
                                  ALU.mult, ALU.add).then_inc(r_ms, 1)
                dve.wait_ge(r_rt, h + 1)
                dve.reciprocal(rss[:, 3, :], rss[:, 2, :]).then_inc(r_rg, 1)
                dve.wait_ge(r_rg, h * 2 + 1)
                dve.tensor_scalar(rss[:, 3, :], rss[:, 3, :], rc[:, P + 1:P + 2], None, ALU.mult).then_inc(r_rg, 1)
                dve.wait_ge(r_rg, h * 2 + 2)
                for q in range(2):
                    o = ro[:, 4 * q:4 * q + 4, :]
                    tt(o, o, rss[:, 3, 4 * q:4 * q + 4].unsqueeze(2).to_broadcast([P, 4, DV]),
                       ALU.mult).then_inc(r_ron, 1)
                ada_sums(first, [15])

                def y_lo(u):
                    q, e = u // 2, u % 2
                    dve.wait_ge(r_yhi, h * 4 + u + 1)
                    lo(half_of(kst[:, e, 1], q), rm[:, u % 2, :], half_of(kst[:, e, 0], q)).then_inc(r_ylo, 1)

                for u in range(4):
                    q, e = u // 2, u % 2
                    dve.wait_ge(r_g, h * 4 + (3, 4)[q])
                    dve.wait_ge(r_rtr, h * 4 + u + 1)
                    if u < 2:
                        dve.wait_ge(r_stlo, h * 2 + 2)
                    else:
                        dve.wait_ge(r_ylo, h * 4 + u - 1)
                    tt(rm[:, u % 2, :], ps[:, 2 + e, :], half_of(gT[:, e], q), ALU.mult).then_inc(r_ym, 1)
                    if u > 0:
                        y_lo(u - 1)
                y_lo(3)
                if first:
                    dve.wait_ge(s_mod, 2)
                    dve.tensor_copy(modT[:, 3 * KT:5 * KT], ps[:, 0, KT:3 * KT]).then_inc(s_modT, 1)
                    for n in range(4):
                        dve.tensor_copy(grows[:, n * HALF:(n + 1) * HALF], ps[0:1, 4 + n, :]).then_inc(s_row, 1)
                dve.wait_ge(r_acc, h * 16)
                for u in range(16):
                    q, k = u // KT, u % KT
                    if u < 15:
                        dve.wait_ge(r_pj, h * 15 + u + 1)
                    else:
                        dve.wait_ge(w_used[place[7][0]], place[7][1] + 1)
                    o = half_of(macc[:, k], q)
                    if first:
                        if u == 4:
                            dve.wait_ge(s_rowout, 16)
                        dve.tensor_copy(o, ps[:, 4 + u % 4, :]).then_inc(r_acc, 1)
                    else:
                        tt(o, ps[:, 4 + u % 4, :], o, ALU.add).then_inc(r_acc, 1)

            ret_head(0, True)
            with dve.Fori(0, RH - 1) as i:
                ret_head(i + 1, False)

            dve.wait_ge(g_ln, 1)
            dve.tensor_scalar(fz[:, 0, :], fz[:, 0, :], 0.0, None, ALU.min).then_inc(g_scan, 1)
            dve.wait_ge(g_scan, 1)
            tt(fz[:, 2, :], fz[:, 1, :], fz[:, 0, :], ALU.subtract)

            def scan(levels):
                for lv in levels:
                    d = 1 << lv
                    src, dst = (2, 3) if lv % 2 == 0 else (3, 2)
                    if lv == 0:
                        dve.drain()
                    else:
                        dve.wait_ge(g_scan, 2 * lv + 1)
                    dve.tensor_copy(fz[:, dst, 0:d], fz[:, src, 0:d]).then_inc(g_scan, 1)
                    tt(fz[:, dst, d:], fz[:, src, d:], fz[:, src, :S - d], ALU.add).then_inc(g_scan, 1)

            def fox_qk_lo(n, count):
                j, half = n // 2, n % 2
                buf = (fq2, fk2)[j]
                dve.wait_ge(a_qkhi, count)
                dve.scalar_tensor_tensor(out=half_of(buf[:, 1], half), in0=ps[:, half, :],
                                         scalar=DH ** -0.5 if j == 0 else 1.0, in1=f(half_of(buf[:, 0], half)),
                                         op0=ALU.mult, op1=ALU.subtract).then_inc(a_qk, 1)

            scan(range(2))
            fox_qk_lo(0, 1)
            fox_qk_lo(1, 2)
            scan(range(2, 10))
            fox_qk_lo(2, 3)
            fox_qk_lo(3, 4)

            def fox_head(base, h, more):
                def normed(t):
                    at = t * (t + 1) // 2 * P
                    dve.wait_ge(a_e, h * 8 + t + 1)
                    dve.reciprocal(smax[:, 3, t:t + 1], smax[:, 2, t:t + 1]).then_inc(a_r, 1)
                    dve.wait_ge(a_r, h * 8 + t + 1)
                    p = probs[:, at:at + (t + 1) * P]
                    dve.tensor_scalar(p, p, smax[:, 3, t:t + 1], None, ALU.mult).then_inc(a_p, 1)

                def v_lo(q):
                    dve.wait_ge(a_vhi, h * 2 + q + 1)
                    lo(fv2[:, 1, 4 * q:4 * q + 4, :], ps[:, 6 + q, :].rearrange("p (b d) -> p b d", d=P),
                       fv2[:, 0, 4 * q:4 * q + 4, :]).then_inc(a_vlo, 1)

                scores = ps[:, 2:4, :].rearrange("p b c -> p (b c)")
                dve.wait_ge(a_nf, 16 * h + 16)
                for t in range(TT):
                    n, at = (t + 1) * P, t * (t + 1) // 2 * P
                    dve.wait_ge(a_s, h * 8 + t + 1)
                    dve.tensor_copy(smax[:, 4, t:t + 1], ps[:, 2, 0:1])
                    dve.tensor_tensor_reduce(probs[:, at:at + n], scores[:, :n], negf[:, :n], 1.0, -3.0e38,
                                             ALU.add, ALU.max, smax[:, 0, t:t + 1]).then_inc(a_t, 1)
                    dve.wait_ge(a_t, h * 8 + t + 1)
                    dve.tensor_scalar(smax[:, 1, t:t + 1], smax[:, 0, t:t + 1], -1.0, None,
                                      ALU.mult).then_inc(a_neg, 1)
                    if 0 < t <= 5:
                        normed(t - 1)
                v_lo(0)
                v_lo(1)

                def y_lo(g):
                    dve.wait_ge(a_yhi, h * 2 + g + 1)
                    lo(half_of(fy2[:, 1], g), ps[:, 6 + g, :], half_of(fy2[:, 0], g)).then_inc(a_ylo, 1)

                for n, (g, s) in enumerate([(0, s) for s in range(4)] + [(1, s) for s in range(8)]):
                    c0 = max(0, s - 4 * g) * P
                    dve.wait_ge(a_pthi, h * 12 + n + 1)
                    lo(pT2[:, n % 3, 1, c0:], ps[:, 4 + n % 2, c0:], pT2[:, n % 3, 0, c0:]).then_inc(a_ptlo, 1)
                    if n < 3:
                        normed(5 + n)
                    if more and n % 3 == 0 and n > 0:
                        fox_qk_lo(n // 3 - 1, h * 4 + 4 + n // 3)
                    if n == 4:
                        y_lo(0)
                if more:
                    fox_qk_lo(3, h * 4 + 8)
                slot, turn = slot_turn(base, 3 if more else 1, h, FOX_TILES)
                for u in range(16):
                    q, k = u // KT, u % KT
                    if u == 2:
                        y_lo(1)
                    if u < 15:
                        dve.wait_ge(a_pj, h * 15 + u + 1)
                    else:
                        dve.wait_ge(w_used[slot], turn + 1)
                    o = half_of(macc[:, k], q)
                    tt(o, ps[:, 2 + u % 4, :], o, ALU.add).then_inc(a_acc, 1)

            dve.memset(begun[:, 0:1], 0.0).then_inc(a_acc, 1)
            dve.wait_ge(s_mzero, KT)
            with dve.Fori(0, FH - 1) as h:
                fox_head(T_FOX, h, True)
            fox_head(T_FOX, FH - 1, False)

            def merge(i, e, s):
                k = 2 * i + e
                dve.wait_ge(o_mret[e], 16 * i + 16)
                for half in range(2):
                    n = 4 * i + 2 * e + half
                    dve.wait_ge(s["ga"], n + 1)
                    tt(ga[:, half, :], ga[:, half, :], half_of(mret[:, e], half), ALU.mult).then_inc(s["gm"], 1)
                for half in range(2):
                    n = 4 * i + 2 * e + half
                    dve.wait_ge(s["gb"], n + 1)
                    m = macc_half(k, half)
                    tt(gb[:, half, :], gb[:, half, :], m, ALU.mult).then_inc(s["gbm"], 1)
                    dve.wait_ge(s["gbm"], n + 1)
                    dve.wait_ge(s["gm"], n + 1)
                    if not (isinstance(i, int) and i == 0 and e == 0):
                        dve.wait_ge(s["lo"], n - 1)
                    tt(fin[:, half, :], ga[:, half, :], gb[:, half, :], ALU.add).then_inc(s["f"], 1)
                for half in range(2):
                    lo_part(i, e, half, s)

            def macc_half(k, half):
                flat = macc[:, :, :].rearrange("p k s -> p (k s)")
                return flat[:, ds(k * S + half * HALF, HALF)]

            def swiglu(i, e, s, place):
                for half in range(2):
                    n = 4 * i + 2 * e + half
                    if half == 0:
                        dve.wait_ge(s["job"], 4 * i + 2 * e + 2)
                    else:
                        dve.wait_ge(w_used[place[0]], place[1] + 1)
                    dve.wait_ge(s["ga"], n + 1)
                    if not (isinstance(i, int) and i == 0 and e == 0):
                        dve.wait_ge(s["lo"], n - 1)
                    tt(fin[:, half, :], ps[:, 2 + half, :], ga[:, half, :], ALU.mult).then_inc(s["f"], 1)
                for half in range(2):
                    lo_part(i, e, half, s)

            def lo_part(i, e, half, s):
                dve.wait_ge(s["hi"], 4 * i + 2 * e + half + 1)
                lo(half_of(f2[:, e, 1], half), fin[:, half, :], half_of(f2[:, e, 0], half)).then_inc(s["lo"], 1)

            def add_second(i, s, place, after=None):
                for u in range(16):
                    t, q = u // 2, u % 2
                    if u < 15:
                        dve.wait_ge(s["pj"], 15 * i + u + 1)
                    else:
                        dve.wait_ge(w_used[place[0]], place[1] + 1)
                    o = half_of(resid[:, t], q)
                    tt(o, ps[:, 4 + u % 4, :], o, ALU.add).then_inc(s["acc"], 1)
                    if after and q == 1:
                        after(t)

            def pair_dve(base, pairs, s, body, after):
                col = 1 if base == T_WO else 2
                dve.memset(begun[:, col:col + 1], 0.0).then_inc(s["acc"], 1)
                first = [slot_turn(base, j) for j in range(4)]
                body(0, 0, s, first[1])
                body(0, 1, s, first[3])

                def later(p, base, j0, it=0, per=0):
                    place = [slot_turn(base, j0 + j, it, per) for j in range(PAIR_TILES)]
                    add_second(p - 1, s, place[2])
                    body(p, 0, s, place[3])
                    body(p, 1, s, place[5])

                later_pairs(dve, base, pairs, later)
                end = base + 4 + PAIR_TILES * (pairs - 1)
                add_second(pairs - 1, s, slot_turn(end, 1), after)

            dve.scalar_tensor_tensor(out=amul[:, :], in0=modT[:, 4 * KT:5 * KT], scalar=1.0, in1=nw[:, 1, :],
                                     op0=ALU.add, op1=ALU.mult).then_inc(s_amul, 1)
            dve.wait_ge(s_x, 32)
            pair_dve(T_WO, KT // 2, pair_sems["o"], lambda i, e, s, place: merge(i, e, s),
                     lambda t: norm_steps(1, t))
            for t in range(TT, TT + 2):
                norm_steps(1, t)
            dve.wait_ge(s_amul, 2)
            modulate(1, 3 * KT, ntmp)

            def last_rows(t):
                if t == 0:
                    dve.wait_ge(s_nf, 16)
                dve.wait_ge(n_r, 2 * TT + t + 1)
                dve.scalar_tensor_tensor(out=resid[:, t, :], in0=resid[:, t, :], scalar=stat[:, 3, t:t + 1],
                                         in1=nfrow[:, :], op0=ALU.mult, op1=ALU.mult).then_inc(f_y, 1)

            pair_dve(T_FFN, FF_PAIRS, pair_sems["f"], swiglu, lambda t: norm_steps(2, t, last_rows))
            for t in range(TT, TT + 3):
                norm_steps(2, t, last_rows)


_INS = ["x", "c", "ada_w", "ada_b", "norm1_w", "w_in", "b_f", "ret_proj", "fox_proj", "w_out",
        "norm2_w", "w_gate", "w_up", "w_down", "norm_f_w"]


def kernel(**inputs):
    import concourse.bacc as bacc
    from concourse.bass_utils import run_bass_kernel_spmd

    nc = bacc.Bacc("TRN2", target_bir_lowering=False, num_devices=1, dynamic_dma_scratch_size=1024)
    arrays = {n: np.ascontiguousarray(inputs[n]) for n in _INS}
    for n in ("c", "norm1_w", "norm2_w"):
        arrays[n] = np.ascontiguousarray(arrays[n].reshape(KT, P).T)
    arrays["b_f"] = arrays["b_f"].reshape(FH, 1)
    arrays.update({"k_" + n: a for n, a in host_constants().items()})
    feeds, args = {}, []
    for name, a in arrays.items():
        feeds[f"in_{name}"] = a
        args.append(nc.dram_tensor(f"in_{name}", a.shape, mybir.dt.from_np(a.dtype), kind="ExternalInput").ap())
    out = nc.dram_tensor("out_0", (1, S, D), F32, kind="ExternalOutput").ap()
    hybrid_block(nc, *args, out)
    return run_bass_kernel_spmd(nc, [feeds], core_ids=[0]).results[0]["out_0"]
```
